# Optimizing a Trainium2 kernel written in Bass

```python
import math
import jax, jax.numpy as jnp
from jax import lax
import numpy as np

D_MODEL = 1024
BATCH = 1
SEQ = 512
DEPTH = 2

GRID_W = 64
CTX_LEN = 256
N_MIXERS = 2
NORM_EPS = 1e-6

DN_QK_HEADS = 8
DN_V_HEADS = 16
DN_HEAD_K = 128
DN_HEAD_V = 128
DN_KEY_DIM = DN_QK_HEADS * DN_HEAD_K
DN_VAL_DIM = DN_V_HEADS * DN_HEAD_V
DN_CONV_DIM = 2 * DN_KEY_DIM + DN_VAL_DIM
DN_CONV_K = 5
DN_CHUNK = 64
DN_IN_DIM = DN_CONV_DIM + DN_VAL_DIM + 4 * DN_V_HEADS
DT_MIN = 0.001
DT_MAX = 0.1

ATT_Q_HEADS = 8
ATT_KV_HEADS = 2
ATT_HEAD_DIM = 128
ATT_Q_DIM = ATT_Q_HEADS * ATT_HEAD_DIM
ATT_KV_DIM = ATT_KV_HEADS * ATT_HEAD_DIM
ATT_IN_DIM = ATT_Q_DIM + 2 * ATT_KV_DIM + ATT_Q_DIM
ATT_BLOCK = 128
ROPE_THETA = 10000.0

N_DN_LAYERS = (DEPTH + N_MIXERS - 1) // N_MIXERS
N_ATT_LAYERS = DEPTH // N_MIXERS


F32 = jnp.float32

def rms_norm(x, g):
    xf = x.astype(F32)
    y = xf * lax.rsqrt(jnp.mean(xf * xf, axis=-1, keepdims=True) + NORM_EPS)
    return (y * g.astype(F32)).astype(x.dtype)

def l2_norm(x):
    xf = x.astype(F32)
    return (xf * lax.rsqrt(jnp.sum(xf * xf, axis=-1, keepdims=True) + NORM_EPS)).astype(x.dtype)

def centred_dwconv(x, w):
    k = w.shape[0]
    return lax.conv_general_dilated(x, w[:, None, :].astype(x.dtype), window_strides=(1,),
                                    padding=[(k // 2, k // 2)],
                                    dimension_numbers=('NWC', 'WIO', 'NWC'),
                                    feature_group_count=x.shape[-1])

def chunk_gated_delta(q, k, v, g, beta, s0):
    b, h, l, dk = k.shape
    dv = v.shape[-1]
    n = l // DN_CHUNK
    q = q.astype(F32) * (dk ** -0.5)
    k = k.astype(F32)
    v32 = v.astype(F32)
    ch = lambda t: t.reshape(b, h, n, DN_CHUNK, *t.shape[3:])
    qc, kc, vc = ch(q), ch(k), ch(v32)
    gc = jnp.cumsum(ch(g.astype(F32)), axis=-1)
    bc = ch(beta.astype(F32))
    idx = jnp.arange(DN_CHUNK)
    lower = idx[:, None] >= idx[None, :]
    strict = idx[:, None] > idx[None, :]
    decay = jnp.exp(jnp.where(lower, gc[..., :, None] - gc[..., None, :], -jnp.inf))
    kb = kc * bc[..., None]
    vb = vc * bc[..., None]
    a = jnp.where(strict, jnp.einsum('bhncd,bhnsd->bhncs', kb, kc) * decay, 0.0)
    eye = jnp.eye(DN_CHUNK, dtype=F32)
    t_inv = lax.linalg.triangular_solve(eye + a, jnp.broadcast_to(eye, a.shape),
                                        left_side=True, lower=True, unit_diagonal=True)
    u = jnp.einsum('bhncs,bhnse->bhnce', t_inv, vb)
    w = jnp.einsum('bhncs,bhnsd->bhncd', t_inv, kb * jnp.exp(gc)[..., None])
    qk = jnp.einsum('bhncd,bhnsd->bhncs', qc, kc) * decay
    q_dec = qc * jnp.exp(gc)[..., None]
    k_dec = kc * jnp.exp(gc[..., -1:] - gc)[..., None]
    g_last = jnp.exp(gc[..., -1])

    def step(s, xs):
        qk_i, qd_i, kd_i, u_i, w_i, gl_i = xs
        v_new = u_i - jnp.einsum('bhcd,bhde->bhce', w_i, s)
        o = jnp.einsum('bhcd,bhde->bhce', qd_i, s) + jnp.einsum('bhcs,bhse->bhce', qk_i, v_new)
        s = s * gl_i[..., None, None] + jnp.einsum('bhcd,bhce->bhde', kd_i, v_new)
        return s, o

    xs = tuple(jnp.moveaxis(t_, 2, 0) for t_ in (qk, q_dec, k_dec, u, w, g_last))
    s_fin, o = lax.scan(step, s0.astype(F32), xs)
    o = jnp.moveaxis(o, 0, 2).reshape(b, h, l, dv)
    return o.astype(v.dtype), s_fin

def bidir_delta(q, k, v, g, beta, s0_f, s0_b):
    o_f, s_f = chunk_gated_delta(q, k, v, g[:, 0], beta[:, 0], s0_f)
    fl = lambda t: jnp.flip(t, axis=2)
    o_b, s_b = chunk_gated_delta(fl(q), fl(k), fl(v), fl(g[:, 1]), fl(beta[:, 1]), s0_b)
    return o_f + fl(o_b), s_f, s_b

def deltanet_mixer(u_lat, u_ctx, w_in, conv_w, a_log, dt_bias, o_norm_g, w_out, need_ctx):
    def branch_inputs(u):
        b, l, _ = u.shape
        p = u @ w_in
        qkv = jax.nn.silu(centred_dwconv(p[..., :DN_CONV_DIM], conv_w))
        z = p[..., DN_CONV_DIM:DN_CONV_DIM + DN_VAL_DIM]
        ab = p[..., DN_CONV_DIM + DN_VAL_DIM:].reshape(b, l, 2, 2, DN_V_HEADS).astype(F32)
        q, k, v = jnp.split(qkv, [DN_KEY_DIM, 2 * DN_KEY_DIM], axis=-1)
        rep = DN_V_HEADS // DN_QK_HEADS
        q = jnp.repeat(l2_norm(q.reshape(b, l, DN_QK_HEADS, DN_HEAD_K)), rep, axis=2)
        k = jnp.repeat(l2_norm(k.reshape(b, l, DN_QK_HEADS, DN_HEAD_K)), rep, axis=2)
        v = v.reshape(b, l, DN_V_HEADS, DN_HEAD_V)
        beta = jax.nn.sigmoid(ab[:, :, 0])
        g = -jnp.exp(a_log.astype(F32)) * jax.nn.softplus(ab[:, :, 1] + dt_bias.astype(F32))
        bhl = lambda t: jnp.transpose(t, (0, 2, 1, 3))
        return bhl(q), bhl(k), bhl(v), jnp.transpose(g, (0, 2, 3, 1)), jnp.transpose(beta, (0, 2, 3, 1)), z

    def finish(o, z):
        b, h, l, dv = o.shape
        o = rms_norm(jnp.transpose(o, (0, 2, 1, 3)), o_norm_g).astype(z.dtype)
        return (o.reshape(b, l, DN_VAL_DIM) * jax.nn.silu(z)) @ w_out

    qc, kc, vc, gc, bc, zc = branch_inputs(u_ctx)
    s_zero = jnp.zeros((u_ctx.shape[0], DN_V_HEADS, DN_HEAD_K, DN_HEAD_V), F32)
    o_ctx, s_f, s_b = bidir_delta(qc, kc, vc, gc, bc, s_zero, s_zero)
    ql, kl, vl, gl, bl, zl = branch_inputs(u_lat)
    o_lat, _, _ = bidir_delta(ql, kl, vl, gl, bl, s_f, s_b)
    y_lat = finish(o_lat, zl)
    y_ctx = finish(o_ctx, zc) if need_ctx else None
    return y_lat, y_ctx

def axial_rope_angles(n):
    rows = n // GRID_W
    row = jnp.broadcast_to(jnp.arange(rows)[:, None], (rows, GRID_W)).reshape(-1).astype(F32)
    col = jnp.broadcast_to(jnp.arange(GRID_W)[None, :], (rows, GRID_W)).reshape(-1).astype(F32)
    axis_dim = ATT_HEAD_DIM // 2
    inv = ROPE_THETA ** (-jnp.arange(0, axis_dim, 2, dtype=F32) / axis_dim)
    return row[:, None] * inv, col[:, None] * inv

def rope_rotate(x, ang):
    x1, x2 = jnp.split(x, 2, axis=-1)
    cos = jnp.cos(ang)[:, None, :].astype(x.dtype)
    sin = jnp.sin(ang)[:, None, :].astype(x.dtype)
    return jnp.concatenate([x1 * cos - x2 * sin, x2 * cos + x1 * sin], axis=-1)

def apply_axial_rope(x, ang_r, ang_c):
    xr, xc = jnp.split(x, 2, axis=-1)
    return jnp.concatenate([rope_rotate(xr, ang_r), rope_rotate(xc, ang_c)], axis=-1)

def gqa_attend(q, k, v):
    b, lq, hq, d = q.shape
    qg = q.reshape(b, lq, ATT_KV_HEADS, hq // ATT_KV_HEADS, d)
    s = jnp.einsum('bqhgd,bkhd->bhgqk', qg, k).astype(F32) * (d ** -0.5)
    p = jax.nn.softmax(s, axis=-1).astype(v.dtype)
    return jnp.einsum('bhgqk,bkhd->bqhgd', p, v).reshape(b, lq, hq, d)

def blocked_gqa(q, k, v):
    b, lq, hq, d = q.shape
    nb = lq // ATT_BLOCK
    qb = jnp.moveaxis(q.reshape(b, nb, ATT_BLOCK, hq, d), 1, 0)
    ob = lax.map(lambda qi: gqa_attend(qi, k, v), qb)
    return jnp.moveaxis(ob, 0, 1).reshape(b, lq, hq, d)

def attention_mixer(u_lat, u_ctx, w_in, q_norm_g, k_norm_g, w_out, need_ctx):
    def project(u):
        b, l, _ = u.shape
        p = u @ w_in
        q, k, v, z = jnp.split(p, [ATT_Q_DIM, ATT_Q_DIM + ATT_KV_DIM, ATT_Q_DIM + 2 * ATT_KV_DIM], axis=-1)
        q = rms_norm(q.reshape(b, l, ATT_Q_HEADS, ATT_HEAD_DIM), q_norm_g)
        k = rms_norm(k.reshape(b, l, ATT_KV_HEADS, ATT_HEAD_DIM), k_norm_g)
        v = v.reshape(b, l, ATT_KV_HEADS, ATT_HEAD_DIM)
        return q, k, v, z

    def finish(o, z):
        b, l = o.shape[:2]
        return (o.reshape(b, l, ATT_Q_DIM) * jax.nn.silu(z)) @ w_out

    qc, kc, vc, zc = project(u_ctx)
    ql, kl, vl, zl = project(u_lat)
    ang_r, ang_c = axial_rope_angles(u_lat.shape[1])
    ql = apply_axial_rope(ql, ang_r, ang_c)
    kl = apply_axial_rope(kl, ang_r, ang_c)
    k_all = jnp.concatenate([kc, kl], axis=1)
    v_all = jnp.concatenate([vc, vl], axis=1)
    y_lat = finish(blocked_gqa(ql, k_all, v_all), zl)
    y_ctx = finish(gqa_attend(qc, kc, vc), zc) if need_ctx else None
    return y_lat, y_ctx

def first_inputs(seed: int = 0) -> dict:
    key = jax.random.key(seed)
    ks = jax.random.split(key, 20)
    nrm = lambda k, shape, scale: jax.random.normal(k, shape, F32) * scale
    d = D_MODEL
    n_dn, n_att = N_DN_LAYERS, N_ATT_LAYERS
    a_log = jnp.log(jax.random.uniform(ks[8], (n_dn, 2, DN_V_HEADS), F32, 1.0, 16.0))
    dt = jnp.exp(jax.random.uniform(ks[9], (n_dn, 2, DN_V_HEADS), F32, math.log(DT_MIN), math.log(DT_MAX)))
    dt_bias = dt + jnp.log(-jnp.expm1(-dt))
    return {
        'x': nrm(ks[0], (BATCH, SEQ, d), 1.0),
        'c': nrm(ks[1], (BATCH, d), 1.0),
        'ctx': nrm(ks[2], (BATCH, CTX_LEN, d), 1.0),
        'c_ctx': nrm(ks[3], (d,), 1.0),
        'norm_g': 1.0 + nrm(ks[4], (DEPTH, d), 0.02),
        'ada_w': nrm(ks[5], (DEPTH, d, 3 * d), 0.5 * d ** -0.5),
        'ada_b': nrm(ks[6], (DEPTH, 3 * d), 0.02),
        'dn_w_in': nrm(ks[7], (n_dn, d, DN_IN_DIM), d ** -0.5),
        'dn_conv_w': nrm(ks[10], (n_dn, DN_CONV_K, DN_CONV_DIM), DN_CONV_K ** -0.5),
        'dn_a_log': a_log,
        'dn_dt_bias': dt_bias,
        'dn_o_norm_g': 1.0 + nrm(ks[11], (n_dn, DN_HEAD_V), 0.02),
        'dn_w_out': nrm(ks[12], (n_dn, DN_VAL_DIM, d), DN_VAL_DIM ** -0.5),
        'att_w_in': nrm(ks[13], (n_att, d, ATT_IN_DIM), d ** -0.5),
        'att_q_norm_g': 1.0 + nrm(ks[14], (n_att, ATT_HEAD_DIM), 0.02),
        'att_k_norm_g': 1.0 + nrm(ks[15], (n_att, ATT_HEAD_DIM), 0.02),
        'att_w_out': nrm(ks[16], (n_att, ATT_Q_DIM, d), ATT_Q_DIM ** -0.5),
        'final_norm_g': 1.0 + nrm(ks[17], (d,), 0.02),
    }

def first_block(x, c, ctx, c_ctx, norm_g, ada_w, ada_b, dn_w_in, dn_conv_w, dn_a_log, dn_dt_bias,
              dn_o_norm_g, dn_w_out, att_w_in, att_q_norm_g, att_k_norm_g, att_w_out, final_norm_g):
    h_lat, h_ctx = x, ctx
    sc_lat, sc_ctx = jax.nn.silu(c), jax.nn.silu(c_ctx)
    for i in range(DEPTH):
        need_ctx = i < DEPTH - 1
        shift, scale, gate = jnp.split(sc_lat @ ada_w[i] + ada_b[i], 3, axis=-1)
        shift_c, scale_c, gate_c = jnp.split(sc_ctx @ ada_w[i] + ada_b[i], 3, axis=-1)
        u_lat = rms_norm(h_lat, norm_g[i]) * (1.0 + scale[:, None]) + shift[:, None]
        u_ctx = rms_norm(h_ctx, norm_g[i]) * (1.0 + scale_c) + shift_c
        j = i // N_MIXERS
        if i % N_MIXERS == 0:
            y_lat, y_ctx = deltanet_mixer(u_lat, u_ctx, dn_w_in[j], dn_conv_w[j], dn_a_log[j], dn_dt_bias[j],
                                          dn_o_norm_g[j], dn_w_out[j], need_ctx)
        else:
            y_lat, y_ctx = attention_mixer(u_lat, u_ctx, att_w_in[j], att_q_norm_g[j], att_k_norm_g[j],
                                           att_w_out[j], need_ctx)
        h_lat = h_lat + gate[:, None] * y_lat
        if need_ctx:
            h_ctx = h_ctx + gate_c * y_ctx
    return rms_norm(h_lat, final_norm_g)


DEPTH_2 = 1

N_MEM = 256
MAX_POS_OFFSET = 1024
BLOCK = 128
RMS_EPS = 1e-6
NEG_INF = -1e30

MLA_HEADS = 8
MLA_NOPE = 64
MLA_ROPE = 32
MLA_V = 64
MLA_QK_DIM = MLA_NOPE + MLA_ROPE
MLA_Q_RANK = 384
MLA_KV_RANK = 256
MLA_WIDTH = MLA_HEADS * MLA_V

DIL_PAIRS = ((128, 1), (512, 4), (2048, 16))
DIL_GROUPS = 3
DIL_HEADS_PER_GROUP = 4
DIL_HEADS = DIL_GROUPS * DIL_HEADS_PER_GROUP
DIL_HEAD_DIM = 128
DIL_WIDTH = DIL_HEADS_PER_GROUP * DIL_HEAD_DIM

MEM_HEADS = 4
MEM_HEAD_DIM = 128
MEM_WIDTH = MEM_HEADS * MEM_HEAD_DIM

N_BRANCH = 3

D_FF = 2816
CONV_WIDTH = 3

OFF_Q = MLA_Q_RANK
OFF_KV = OFF_Q + MLA_KV_RANK
OFF_KR = OFF_KV + MLA_ROPE
OFF_DIL = OFF_KR + 3 * DIL_HEADS * DIL_HEAD_DIM
OFF_MEMQ = OFF_DIL + MEM_WIDTH
D_IN = OFF_MEMQ + N_BRANCH * D_MODEL


def _rms_norm(x, g):
    xf = x.astype(jnp.float32)
    y = xf * lax.rsqrt(jnp.mean(xf * xf, axis=-1, keepdims=True) + RMS_EPS)
    return (y * g.astype(jnp.float32)).astype(x.dtype)

def _rope(t, positions):
    half = t.shape[-1] // 2
    inv_freq = ROPE_THETA ** (-jnp.arange(half, dtype=jnp.float32) / half)
    ang = positions.astype(jnp.float32)[:, :, None, None] * inv_freq
    cos, sin = jnp.cos(ang), jnp.sin(ang)
    t1 = t[..., :half].astype(jnp.float32)
    t2 = t[..., half:].astype(jnp.float32)
    return jnp.concatenate([t1 * cos - t2 * sin, t2 * cos + t1 * sin], axis=-1).astype(t.dtype)

def _alibi_slopes(n):
    return jnp.exp2(-8.0 * jnp.arange(1, n + 1, dtype=jnp.float32) / n)

def _mla(c_q, c_kv, k_rope, positions, q_norm, w_uq, kv_norm, w_ukv):
    B, S, _ = c_q.shape
    q = (_rms_norm(c_q, q_norm) @ w_uq).reshape(B, S, MLA_HEADS, MLA_QK_DIM)
    q = jnp.concatenate([q[..., :MLA_NOPE], _rope(q[..., MLA_NOPE:], positions)], axis=-1)
    kv = (_rms_norm(c_kv, kv_norm) @ w_ukv).reshape(B, S, MLA_HEADS, MLA_NOPE + MLA_V)
    k_pe = jnp.broadcast_to(_rope(k_rope[:, :, None, :], positions), (B, S, MLA_HEADS, MLA_ROPE))
    k = jnp.concatenate([kv[..., :MLA_NOPE], k_pe], axis=-1)
    v = kv[..., MLA_NOPE:]
    n_blk = S // BLOCK
    q_blocks = (q * MLA_QK_DIM ** -0.5).reshape(B, n_blk, BLOCK, MLA_HEADS, MLA_QK_DIM).transpose(1, 0, 2, 3, 4)
    key_idx = jnp.arange(S)

    def attend(args):
        q_blk, blk = args
        s = jnp.einsum('bqhd,bkhd->bhqk', q_blk, k).astype(jnp.float32)
        q_idx = blk * BLOCK + jnp.arange(BLOCK)
        s = jnp.where(key_idx[None, :] <= q_idx[:, None], s, NEG_INF)
        p = jax.nn.softmax(s, axis=-1).astype(v.dtype)
        return jnp.einsum('bhqk,bkhd->bqhd', p, v)

    o = lax.map(attend, (q_blocks, jnp.arange(n_blk)))
    return o.transpose(1, 0, 2, 3, 4).reshape(B, S, MLA_WIDTH)

def _dilated_group(q, k, v, window, dilation, slopes):
    B, S, H, dh = q.shape
    span = window // dilation
    L = S // dilation
    n_blk = -(-L // BLOCK)
    Lp = n_blk * BLOCK

    def to_blocks(t):
        t = t.reshape(B, L, dilation, H, dh).transpose(0, 2, 3, 1, 4)
        t = jnp.pad(t, ((0, 0), (0, 0), (0, 0), (0, Lp - L), (0, 0)))
        return t.reshape(B, dilation, H, n_blk, BLOCK, dh)

    def band(t):
        prev = jnp.pad(t, ((0, 0), (0, 0), (0, 0), (1, 0), (0, 0), (0, 0)))[:, :, :, :-1]
        return jnp.concatenate([prev, t], axis=4)

    qb = to_blocks(q) * dh ** -0.5
    kb = band(to_blocks(k))
    vb = band(to_blocks(v))
    s = jnp.einsum('bdhnqe,bdhnke->bdhnqk', qb, kb).astype(jnp.float32)
    dist = jnp.arange(BLOCK)[:, None] + BLOCK - jnp.arange(2 * BLOCK)[None, :]
    key_sub = jnp.arange(n_blk)[:, None, None] * BLOCK - BLOCK + jnp.arange(2 * BLOCK)[None, None, :]
    valid = (dist >= 0) & (dist <= span) & (key_sub >= 0)
    alibi = -slopes.astype(jnp.float32)[:, None, None, None] * (dist * dilation).astype(jnp.float32)
    s = jnp.where(valid, s + alibi, NEG_INF)
    m = jnp.max(s, axis=-1, keepdims=True)
    e = jnp.exp(s - m)
    den = jnp.sum(e, axis=-1, keepdims=True)
    o = jnp.einsum('bdhnqk,bdhnke->bdhnqe', (e / den).astype(v.dtype), vb)
    lse = (m + jnp.log(den))[..., 0]
    o = o.reshape(B, dilation, H, Lp, dh)[:, :, :, :L].transpose(0, 3, 1, 2, 4).reshape(B, S, H, dh)
    lse = lse.reshape(B, dilation, H, Lp)[..., :L].transpose(0, 3, 1, 2).reshape(B, S, H)
    return o, lse

def _dilated_mixture(dil_qkv):
    B, S, _ = dil_qkv.shape
    qkv = dil_qkv.reshape(B, S, 3, DIL_GROUPS, DIL_HEADS_PER_GROUP, DIL_HEAD_DIM)
    slopes = _alibi_slopes(DIL_HEADS).reshape(DIL_HEADS_PER_GROUP, DIL_GROUPS).T
    outs, lses = [], []
    for g, (window, dilation) in enumerate(DIL_PAIRS):
        o, lse = _dilated_group(qkv[:, :, 0, g], qkv[:, :, 1, g], qkv[:, :, 2, g], window, dilation, slopes[g])
        outs.append(o)
        lses.append(lse)
    w = jax.nn.softmax(jnp.stack(lses, axis=0), axis=0)
    o_stack = jnp.stack(outs, axis=0)
    o = jnp.sum(w[..., None].astype(o_stack.dtype) * o_stack, axis=0)
    return o.reshape(B, S, DIL_WIDTH)

def _mem_attention(q, mem, g_mem, w_mem_kv):
    B, S, _ = q.shape
    M = mem.shape[1]
    kv = (_rms_norm(mem, g_mem) @ w_mem_kv).reshape(B, M, 2, MEM_HEADS, MEM_HEAD_DIM)
    qh = q.reshape(B, S, MEM_HEADS, MEM_HEAD_DIM) * MEM_HEAD_DIM ** -0.5
    s = jnp.einsum('bshd,bmhd->bhsm', qh, kv[:, :, 0]).astype(jnp.float32)
    p = jax.nn.softmax(s, axis=-1).astype(q.dtype)
    return jnp.einsum('bhsm,bmhd->bshd', p, kv[:, :, 1]).reshape(B, S, MEM_WIDTH)

def _conv_ffn(h, w_up, conv_w, conv_b, w_down):
    S = h.shape[1]
    u = h @ w_up
    u_pad = jnp.pad(u, ((0, 0), (CONV_WIDTH - 1, 0), (0, 0)))
    z = conv_b + conv_w[0] * u_pad[:, 0:S]
    for j in range(1, CONV_WIDTH):
        z = z + conv_w[j] * u_pad[:, j:j + S]
    gate, val = z[..., :D_FF], z[..., D_FF:]
    return (jax.nn.silu(gate) * val) @ w_down

def _layer(x, mem, positions, g_pre_mix, w_in, b_gate, mla_q_norm, w_uq, mla_kv_norm, w_ukv, g_mem, w_mem_kv,
           w_br_mla, w_br_dil, w_br_mem, w_o, g_post_mix, g_pre_ffn, w_ffn_up, conv_w, conv_b, w_ffn_down, g_post_ffn):
    B, S, _ = x.shape
    h = _rms_norm(x, g_pre_mix)
    proj = h @ w_in
    y_mla = _mla(proj[..., :OFF_Q], proj[..., OFF_Q:OFF_KV], proj[..., OFF_KV:OFF_KR], positions,
                 mla_q_norm, w_uq, mla_kv_norm, w_ukv)
    y_dil = _dilated_mixture(proj[..., OFF_KR:OFF_DIL])
    y_mem = _mem_attention(proj[..., OFF_DIL:OFF_MEMQ], mem, g_mem, w_mem_kv)
    gates = jax.nn.sigmoid((proj[..., OFF_MEMQ:] + b_gate).astype(jnp.float32)).astype(x.dtype)
    gates = gates.reshape(B, S, N_BRANCH, D_MODEL)
    merged = (gates[:, :, 0] * (y_mla @ w_br_mla)
              + gates[:, :, 1] * (y_dil @ w_br_dil)
              + gates[:, :, 2] * (y_mem @ w_br_mem))
    x = x + _rms_norm(merged @ w_o, g_post_mix)
    h2 = _rms_norm(x, g_pre_ffn)
    x = x + _rms_norm(_conv_ffn(h2, w_ffn_up, conv_w, conv_b, w_ffn_down), g_post_ffn)
    return x

def second_inputs(seed: int = 0) -> dict:
    key = jax.random.key(seed)
    ks = jax.random.split(key, 24)
    f32 = jnp.float32

    def dense(k, fan_in, fan_out):
        return jax.random.normal(k, (DEPTH_2, fan_in, fan_out), f32) * fan_in ** -0.5

    def gain(k, n):
        return 1.0 + 0.05 * jax.random.normal(k, (DEPTH_2, n), f32)

    x = jax.random.normal(ks[0], (BATCH, SEQ, D_MODEL), f32)
    mem = jax.random.normal(ks[1], (BATCH, N_MEM, D_MODEL), f32)
    offset = jax.random.randint(ks[2], (BATCH, 1), 0, MAX_POS_OFFSET, dtype=jnp.int32)
    positions = (offset + jnp.arange(SEQ, dtype=jnp.int32)[None, :]).astype(jnp.int32)
    return {
        "x": x,
        "mem": mem,
        "positions": positions,
        "g_pre_mix": gain(ks[3], D_MODEL),
        "w_in": dense(ks[4], D_MODEL, D_IN),
        "b_gate": 0.1 * jax.random.normal(ks[5], (DEPTH_2, N_BRANCH * D_MODEL), f32),
        "mla_q_norm": gain(ks[6], MLA_Q_RANK),
        "w_uq": dense(ks[7], MLA_Q_RANK, MLA_HEADS * MLA_QK_DIM),
        "mla_kv_norm": gain(ks[8], MLA_KV_RANK),
        "w_ukv": dense(ks[9], MLA_KV_RANK, MLA_HEADS * (MLA_NOPE + MLA_V)),
        "g_mem": gain(ks[10], D_MODEL),
        "w_mem_kv": dense(ks[11], D_MODEL, 2 * MEM_WIDTH),
        "w_br_mla": dense(ks[12], MLA_WIDTH, D_MODEL),
        "w_br_dil": dense(ks[13], DIL_WIDTH, D_MODEL),
        "w_br_mem": dense(ks[14], MEM_WIDTH, D_MODEL),
        "w_o": dense(ks[15], D_MODEL, D_MODEL),
        "g_post_mix": gain(ks[16], D_MODEL),
        "g_pre_ffn": gain(ks[17], D_MODEL),
        "w_ffn_up": dense(ks[18], D_MODEL, 2 * D_FF),
        "conv_w": jax.random.normal(ks[19], (DEPTH_2, CONV_WIDTH, 2 * D_FF), f32) * CONV_WIDTH ** -0.5,
        "conv_b": 0.01 * jax.random.normal(ks[20], (DEPTH_2, 2 * D_FF), f32),
        "w_ffn_down": dense(ks[21], D_FF, D_MODEL),
        "g_post_ffn": gain(ks[22], D_MODEL),
    }

def second_block(x, mem, positions, g_pre_mix, w_in, b_gate, mla_q_norm, w_uq, mla_kv_norm, w_ukv, g_mem, w_mem_kv,
              w_br_mla, w_br_dil, w_br_mem, w_o, g_post_mix, g_pre_ffn, w_ffn_up, conv_w, conv_b, w_ffn_down,
              g_post_ffn):
    for l in range(DEPTH_2):
        x = _layer(x, mem, positions, g_pre_mix[l], w_in[l], b_gate[l], mla_q_norm[l], w_uq[l], mla_kv_norm[l],
                   w_ukv[l], g_mem[l], w_mem_kv[l], w_br_mla[l], w_br_dil[l], w_br_mem[l], w_o[l], g_post_mix[l],
                   g_pre_ffn[l], w_ffn_up[l], conv_w[l], conv_b[l], w_ffn_down[l], g_post_ffn[l])
    return x


def setup_inputs(seed=0):
    out = dict(first_inputs(seed))
    for name, value in second_inputs(seed + 1).items():
        if name != "x":
            out[name + "_2"] = value
    return out


def reference(
    x, c, ctx, c_ctx, norm_g, ada_w, ada_b, dn_w_in, dn_conv_w, dn_a_log, dn_dt_bias,
    dn_o_norm_g, dn_w_out, att_w_in, att_q_norm_g, att_k_norm_g, att_w_out, final_norm_g, mem_2,
    positions_2, g_pre_mix_2, w_in_2, b_gate_2, mla_q_norm_2, w_uq_2, mla_kv_norm_2, w_ukv_2,
    g_mem_2, w_mem_kv_2, w_br_mla_2, w_br_dil_2, w_br_mem_2, w_o_2, g_post_mix_2, g_pre_ffn_2,
    w_ffn_up_2, conv_w_2, conv_b_2, w_ffn_down_2, g_post_ffn_2,
):
    x = first_block(
        x, c, ctx, c_ctx, norm_g, ada_w, ada_b, dn_w_in, dn_conv_w, dn_a_log, dn_dt_bias,
        dn_o_norm_g, dn_w_out, att_w_in, att_q_norm_g, att_k_norm_g, att_w_out, final_norm_g,
    )
    return second_block(
        x, mem_2, positions_2, g_pre_mix_2, w_in_2, b_gate_2, mla_q_norm_2, w_uq_2,
        mla_kv_norm_2, w_ukv_2, g_mem_2, w_mem_kv_2, w_br_mla_2, w_br_dil_2, w_br_mem_2, w_o_2,
        g_post_mix_2, g_pre_ffn_2, w_ffn_up_2, conv_w_2, conv_b_2, w_ffn_down_2, g_post_ffn_2,
    )


_drawn_inputs = setup_inputs


def setup_inputs(seed=0):
    import zlib

    import numpy as np

    out = dict(_drawn_inputs(seed))
    spreads = {}
    factors = {'norm_g': 6.398,
     'dn_o_norm_g': 8.0,
     'att_q_norm_g': 8.0,
     'att_k_norm_g': 8.0,
     'mla_q_norm_2': 3.714,
     'g_mem_2': 3.301,
     'conv_b_2': 6.98}
    for name, (base, spread) in spreads.items():
        noise = np.random.default_rng([zlib.crc32(name.encode()), seed]).standard_normal(out[name].shape)
        drawn = base * np.exp(spread * noise) if base else spread * noise
        out[name] = __import__('jax').numpy.asarray(drawn.astype(out[name].dtype))
    for name, factor in factors.items():
        out[name] = (out[name] * factor).astype(out[name].dtype)
    return out
```

```python
import math
from contextlib import ExitStack

import numpy as np

import concourse.bass as bass
from concourse import mybir

F32 = mybir.dt.float32
I32 = mybir.dt.int32
ALU = mybir.AluOpType
ACT = mybir.ActivationFunctionType
AX = mybir.AxisListType.X
MUL, ADD, SUB = ALU.mult, ALU.add, ALU.subtract

LN_SET = "natural_log_exp_and_others"
T_ALL, T_CTX, T_LAT = 768, 256, 512
EPS = 1e-6


class Queue:

    def __init__(self, new_sem, name):
        self.new_sem, self.name, self.part = new_sem, name, 0
        self.ops, self.met = [], {}
        self.sem, self.count = new_sem(name + "0"), 0
        self.last = None

    def wait(self, *toks):
        for tok in toks:
            if tok is None:
                continue
            if isinstance(tok, list):
                self.wait(*tok)
                continue
            sem, value = tok
            if self.met.get(id(sem), 0) < value:
                self.met[id(sem)] = value
                self.ops.append(lambda e, s=sem, v=value: e.wait_ge(s, v))

    def do(self, make, *toks, chain=True):
        if self.count >= 30000:
            self.wait(self.last)
            self.part += 1
            self.sem, self.count = self.new_sem(f"{self.name}{self.part}"), 0
        self.wait(*toks)
        if chain:
            self.wait(self.last)
        self.count += 1
        self.ops.append(lambda e, m=make, s=self.sem: m(e).then_inc(s, 1))
        self.last = (self.sem, self.count)
        return self.last

    def quiet(self, make):
        self.ops.append(lambda e, m=make: m(e))

    def dma(self, sem, dst, src, *toks):
        self.wait(*toks)
        sem.count += 16
        self.ops.append(lambda e, d=dst, s=src, h=sem.sem: e.dma_start(d, s).then_inc(h, 16))
        return (sem.sem, sem.count)

    def play(self, e):
        for op in self.ops:
            op(e)


class _Dma:
    def __init__(self, sem):
        self.sem, self.count = sem, 0


def bc(ap, axis, shape):
    return ap.unsqueeze(axis).to_broadcast(shape)



CONST = {}
NCONST = 0
for _name, _w in [("ident", 128), ("ones", 128), ("tri", 256), ("strict", 256), ("mask", 7 * 256),
                  ("perm", 128), ("perm96", 96), ("eps", 1), ("lnq", 1), ("invf", 1)]:
    CONST[_name] = (NCONST, NCONST + _w)
    NCONST += _w


def constants():
    a = np.zeros((128, NCONST), np.float32)
    i = np.arange(128)
    r, c = i[:, None], i[None, :]

    def put(name, value):
        a[:, slice(*CONST[name])] = value

    put("ident", np.eye(128))
    put("ones", 1.0)
    put("tri", np.concatenate([r <= c, r >= c], 1))
    put("strict", np.concatenate([r > c, r < c], 1))
    masks = []
    for b in (2, 4, 8, 16, 32, 64, 128):
        m = ((r // b) == (c // b)) & ((r % b) < b // 2) & ((c % b) >= b // 2)
        masks += [-(m.astype(np.float32)), -(m.T.astype(np.float32))]
    put("mask", np.concatenate(masks, 1))
    rot = np.zeros((128, 128), np.float32)
    for m in range(128):
        if m % 64 < 32:
            rot[m + 32, m] = -1.0
        else:
            rot[m - 32, m] = 1.0
    put("perm", rot)
    rot = np.zeros((128, 96), np.float32)
    for m in range(16):
        rot[80 + m, 64 + m] = -1.0
        rot[64 + m, 80 + m] = 1.0
    put("perm96", rot)
    put("eps", EPS)
    put("lnq", math.log(128.0 ** -0.5))
    invf = np.zeros((128, 1), np.float32)
    f = np.float32(10000.0) ** (-np.arange(16, dtype=np.float32) / np.float32(16))
    invf[64:80, 0] = f
    invf[80:96, 0] = f
    put("invf", invf)
    return a


def axial_tables():
    t = np.arange(512)
    row, col = (t // 64).astype(np.float32), (t % 64).astype(np.float32)
    inv = np.float32(10000.0) ** (-np.arange(0, 64, 2, dtype=np.float32) / np.float32(64))
    ang = np.zeros((128, 512), np.float32)
    for m in range(128):
        ang[m] = (row if m < 64 else col) * inv[m % 32]
    return np.concatenate([np.cos(ang), np.sin(ang)], 1).astype(np.float32)


NEG = -1e30


def bias_tables():
    i = np.arange(128)
    r, c = i[:, None], i[None, :]
    slopes = np.exp2(-8.0 * np.arange(1, 13, dtype=np.float32) / 12).astype(np.float32)
    out = []

    def table(slope, dist, valid, dilation):
        out.append(np.where(valid, -slope * (dist * dilation).astype(np.float32), np.float32(NEG)))

    for h in range(4):
        table(slopes[3 * h], r + 128 - c, c >= r, 1)
        table(slopes[3 * h], r - c, r >= c, 1)
    for h in range(4):
        table(slopes[3 * h + 1], r - c, r >= c, 4)
    for h in range(4):
        table(slopes[3 * h + 2], r - c, (r >= c) & (r // 32 == c // 32), 16)
    out.append(np.zeros((128, 384)))
    out.append(np.where(r >= c, np.float32(0), np.float32(NEG)))
    return np.concatenate(out, 1).astype(np.float32)


VECS = {}
NVEC = 0
for _name, _w in [("ada_b", 48), ("norm_g", 16), ("conv", 160), ("cvec", 16), ("final_g", 8), ("qn_g", 1),
                  ("kn_g", 1), ("pre_mix", 8), ("b_gate", 24), ("mla_q", 3), ("mla_kv", 2), ("g_mem", 8),
                  ("post_mix", 8), ("pre_ffn", 8), ("conv_b", 44), ("conv_w", 132), ("post_ffn", 8)]:
    VECS[_name] = (NVEC, NVEC + _w)
    NVEC += _w


def program(nc, D):
    ctx = ExitStack()
    with ctx:
        def new_sem(name):
            return ctx.enter_context(nc.semaphore(name))

        WORDS = 53200
        arena = ctx.enter_context(nc.sbuf_tensor("arena", [128, WORDS], F32))
        ps = ctx.enter_context(nc.psum_tensor("ps", [128, 8, 512], F32))
        psf = ps[:, :, :].rearrange("p b n -> p (b n)")
        top = [0]

        def take(n):
            a = top[0]
            top[0] += n
            assert top[0] <= WORDS, top[0]
            return arena[:, a:a + n]

        pe, dve, act, pool, sp = (Queue(new_sem, n) for n in ("pe", "dve", "act", "pool", "sp"))

        def dsem(name):
            return _Dma(new_sem(name))

        def mm(out, lhsT, rhs, start, stop):
            pe.quiet(lambda e: e.matmul(out, lhsT, rhs, start=start, stop=stop))

        def mmt(out, lhsT, rhs, start, stop):
            return pe.do(lambda e: e.matmul(out, lhsT, rhs, start=start, stop=stop), chain=False)

        def tr(out, src, n=128):
            pe.quiet(lambda e: e.transpose(out, src, ident[0:n, 0:n]))

        def trt(out, src, n=128):
            return pe.do(lambda e: e.transpose(out, src, ident[0:n, 0:n]), chain=False)

        def vtt(out, a, b, op, *toks):
            return dve.do(lambda e: e.tensor_tensor(out, a, b, op), *toks)

        def vts(out, a, s1, s2, op0, op1, *toks):
            if op1 is None:
                return dve.do(lambda e: e.tensor_scalar(out, a, s1, s2, op0), *toks)
            return dve.do(lambda e: e.tensor_scalar(out, a, s1, s2, op0, op1), *toks)

        def vstt(out, a, s, b, op0, op1, *toks):
            return dve.do(lambda e: e.scalar_tensor_tensor(out, a, s, b, op0, op1), *toks)

        def vcopy(out, a, *toks):
            return dve.do(lambda e: e.tensor_copy(out, a), *toks)

        def ptt(out, a, b, op, *toks):
            return pool.do(lambda e: e.tensor_tensor(out, a, b, op), *toks)

        def aact(out, a, func, *toks, bias=None, scale=None, accum=None):
            kw = {}
            if bias is not None:
                kw["bias"] = bias
            if scale is not None:
                kw["scale"] = scale
            if accum is not None:
                kw["accum_out"] = accum
            return act.do(lambda e: e.activation(out, a, func, **kw), *toks)

        def acopy(out, a, *toks, scale=None):
            return aact(out, a, ACT.Copy, *toks, scale=scale)

        def table(name):
            act.quiet(lambda e: e.preload_act_table_set(name))

        def finish_block():
            block = ctx.enter_context(nc.Block())

            @block.tensor
            def _(e):
                pe.play(e)

            @block.vector
            def _(e):
                dve.play(e)

            @block.scalar
            def _(e):
                act.play(e)

            @block.gpsimd
            def _(e):
                pool.play(e)

            @block.sync
            def _(e):
                sp.play(e)

        cst = take(NCONST)
        vec = take(NVEC)

        def K(name, a=0, b=None):
            lo, hi = CONST[name]
            return cst[:, lo + a:hi if b is None else lo + b]

        def V(name, a=0, b=None):
            lo, hi = VECS[name]
            return vec[:, lo + a:hi if b is None else lo + b]

        ident, ones = K("ident"), K("ones")
        eps = K("eps")
        s_in = dsem("s_in")
        sp.dma(s_in, cst, D["consts"])
        t_in = sp.dma(s_in, vec, D["vecs"])

        RING, SLOT = 2, 4096
        ring = [take(SLOT) for _ in range(RING)]
        ring_sem = [dsem(f"ring{i}") for i in range(RING)]
        ring_free, ring_at = [None] * RING, [0]

        def wload(*parts):
            i = ring_at[0] % len(ring)
            ring_at[0] += 1
            tok, at = None, 0
            for src in parts:
                n = src.shape[1]
                tok = sp.dma(ring_sem[i], ring[i][:, at:at + n], src, ring_free[i])
                at += n
            return i, ring[i], tok

        base = top[0]
        mod = take(2 * 48)
        gA = take(2 * 16)
        mark_0 = top[0]
        uT = take(8 * T_ALL)
        mark_u = top[0]
        hT = take(8 * T_ALL)
        mark_h = top[0]

        s_h = dsem("s_h")
        t_h = sp.dma(s_h, hT, D["xT"])
        sc = take(16)
        row = take(3072)
        t_sc = aact(sc, V("cvec"), ACT.Silu, t_in)
        scv = sc.rearrange("p (k v) -> p k v", v=2)
        t_mod = []
        bank_free = [None] * 8
        for layer in range(2):
            t_row = None
            for n in range(6):
                i, w, t_w = wload(D["ada_w"][layer * 6 + n])
                b = n % 2
                pe.wait(t_sc, t_w, bank_free[b])
                for k in range(8):
                    t = (mmt if k == 7 else mm)(ps[0:2, b, :], scv[:, k, :], w[:, k * 512:(k + 1) * 512],
                                                k == 0, k == 7)
                ring_free[i] = t
                bank_free[b] = acopy(row[0:2, n * 512:(n + 1) * 512], ps[0:2, b, :], t,
                                     bank_free[2] if layer else None)
                t_row = bank_free[b]
            pe.wait(t_row, bank_free[2])
            for c in range(24):
                t = (trt if c == 23 else tr)(ps[:, 2, 2 * c:2 * c + 2], row[0:2, c * 128:(c + 1) * 128], 2)
            m = mod[:, layer * 48:layer * 48 + 48].rearrange("p (c v) -> p c v", v=2)
            t = vtt(m, ps[:, 2, 0:48].rearrange("p (c v) -> p c v", v=2),
                    bc(V("ada_b", layer * 24, layer * 24 + 24), 2, [128, 24, 2]), ADD, t, t_in)
            bank_free[2] = t
            ga = gA[:, layer * 16:layer * 16 + 16].rearrange("p (c v) -> p c v", v=2)
            vts(ga, m[:, 8:16, :], 1.0, None, ADD, None)
            t_mod.append(vtt(ga, ga, bc(V("norm_g", layer * 8, layer * 8 + 8), 2, [128, 8, 2]), MUL))
        table(LN_SET)
        top[0] = mark_h

        def modv(layer, c, v):
            return mod[:, layer * 48 + 2 * c + v:layer * 48 + 2 * c + v + 1]

        def gAv(layer, c, v):
            return gA[:, layer * 16 + 2 * c + v:layer * 16 + 2 * c + v + 1]

        SEGS = [(256, 512, 0), (0, 256, 1)]

        def mean_square(src, n, width, banks, sq, ready, rstd, free, div):
            t = None
            wide = width > 512
            sqt = [None] * len(sq)
            for k in range(n):
                s = sq[k % len(sq)]
                t_sq = aact(s[:, 0:width], src(k), ACT.Square, ready, sqt[k % len(sq)])
                pe.wait(t_sq, free)
                if wide:
                    mm(psf[:, banks * 512:banks * 512 + 512], ones, s[:, 0:512], k == 0, k == n - 1)
                    t = mmt(psf[:, banks * 512 + 512:banks * 512 + width], ones, s[:, 512:width],
                            k == 0, k == n - 1)
                else:
                    t = mmt(psf[:, banks * 512:banks * 512 + width], ones, s[:, 0:width], k == 0, k == n - 1)
                sqt[k % len(sq)] = t
            t1 = aact(rstd, psf[:, banks * 512:banks * 512 + width], ACT.Ln, t, bias=eps, scale=1.0 / div)
            return aact(rstd, rstd, ACT.Exp, scale=-0.5), t1

        rstd = take(T_ALL)
        sq = [take(T_ALL), take(T_ALL)]

        def modulate(layer, out):
            t_r, _ = mean_square(lambda k: hT[:, k * T_ALL:(k + 1) * T_ALL], 8, T_ALL, 3, sq,
                                 [t_h, t_mod, bank_free[3], bank_free[4]], rstd, None, 1024.0)
            t = None
            for k in range(8):
                o = out[:, k * T_ALL:(k + 1) * T_ALL]
                vtt(o, hT[:, k * T_ALL:(k + 1) * T_ALL], rstd, MUL, t_r, t_mod[layer])
                for a, n, v in SEGS:
                    t = vts(o[:, a:a + n], o[:, a:a + n], gAv(layer, k, v), modv(layer, k, v), MUL, ADD)
            return t

        t_u = modulate(0, uT)
        top[0] = mark_u

        gt, beta, eg, neg_eg, kdec, gl = (take(192) for _ in range(6))
        mark_a = top[0]
        dtb, expa = take(32), take(32)
        s_small = dsem("s_small")
        act.dma(s_small, dtb, D["dt_bias"].partition_broadcast(128), t_u)
        t_sm = act.dma(s_small, expa, D["a_log"].partition_broadcast(128))
        i, w, t_w = wload(D["w_ab"])
        pe.wait(t_w, t_u)
        for c in range(6):
            for k in range(8):
                t = (mmt if k == 7 else mm)(ps[:, 0, c * 64:c * 64 + 64],
                                            uT[:, k * T_ALL + c * 128:k * T_ALL + c * 128 + 128],
                                            w[:, k * 64:k * 64 + 64], k == 0, k == 7)
        ring_free[i] = t
        lg = take(384)
        t = acopy(lg, ps[:, 0, 0:384], t, bank_free[0])
        bank_free[0] = t
        lgv = lg.rearrange("p (c a x) -> p c a x", c=6, a=2)
        tmp, tm2 = take(192), take(192)
        tv, t2v = (x.rearrange("p (c x) -> p c x", c=6) for x in (tmp, tm2))
        t = aact(tv, lgv[:, :, 0, :], ACT.Exp, scale=-1.0)
        vts(tmp, tmp, 1.0, None, ADD, None, t)
        dve.do(lambda e: e.reciprocal(beta, tmp))
        t_ea = aact(expa, expa, ACT.Exp, t_sm)
        t = vtt(tv, lgv[:, :, 1, :], bc(dtb, 1, [128, 6, 32]), ADD, t_sm)
        t = aact(tm2, tmp, ACT.Abs, t)
        t = aact(tm2, tm2, ACT.Exp, scale=-1.0)
        t = aact(tm2, tm2, ACT.Ln, bias=K("ones", 0, 1), scale=1.0)
        vstt(tmp, tmp, 0.0, tm2, ALU.max, ADD, t)
        vtt(tv, tv, bc(expa, 1, [128, 6, 32]), MUL, t_ea)
        t_g = vts(gt, tmp, -1.0, None, MUL, None)
        gv = gt.rearrange("p (c d h) -> p d c h", c=6, d=2)
        pe.wait(t_g)
        for d in range(2):
            mm(ps[:, 1, d * 96:d * 96 + 96].rearrange("p (c h) -> p c h", c=6),
               K("tri", d * 128, d * 128 + 128), gv[:, d], True, True)
            mm(ps[:, 1, 192 + d * 96:192 + d * 96 + 96].rearrange("p (c h) -> p c h", c=6),
               K("strict", d * 128, d * 128 + 128), gv[:, d], True, True)
        t = mmt(ps[:, 2, 0:192], ones, gt, True, True)

        def dch(x):
            return x.rearrange("p (c d h) -> p d c h", c=6, d=2)

        for d in range(2):
            aact(dch(eg)[:, d], ps[:, 1, d * 96:d * 96 + 96].rearrange("p (c h) -> p c h", c=6), ACT.Exp, t)
            aact(dch(kdec)[:, d], ps[:, 1, 192 + d * 96:192 + d * 96 + 96].rearrange("p (c h) -> p c h", c=6),
                 ACT.Exp)
        t = aact(gl, ps[:, 2, 0:192], ACT.Exp)
        bank_free[1] = bank_free[2] = t
        t_small = vts(neg_eg, eg, -1.0, None, MUL, None, t)
        top[0] = mark_a

        def cols(x, c, d, h0, n=2):
            a = c * 32 + d * 16 + h0
            return x[:, a:a + n]

        qT = [take(T_ALL) for _ in range(2)]
        kT = [take(T_ALL) for _ in range(2)]
        kN = [take(T_ALL) for _ in range(2)]
        vN = [take(2 * T_ALL) for _ in range(2)]
        zgs = [take(2 * T_ALL) for _ in range(2)]
        onorm = take(128)
        t_on = act.dma(s_small, onorm, D["o_norm_g"].partition_broadcast(128), t_small)
        Yf = take(6 * 512)
        PT = take(6 * 512)
        S = take(512)
        rr, vn, vd, qs = (take(512) for _ in range(4))
        oF, oB = take(6 * 256), take(6 * 256)
        mark_s = top[0]
        raw = [take(774), take(774)]
        cv = [take(770) for _ in range(4)]
        sqA = take(T_ALL)
        rsA = take(T_ALL)
        end_p = top[0]
        top[0] = mark_s
        slots = [[take(512) for _ in range(5)] for _ in range(3)]
        top[0] = max(top[0], end_p)

        def u4(x):
            return x.rearrange("p (d h s) -> p d h s", d=2, h=2)

        prev = {}

        def project(j):
            par, zg = j % 2, zgs[j % 2]
            i, w, t_w = wload(D["w_dn"][j])
            wv = w.rearrange("p (k m) -> p k m", k=8)
            t_c = []
            for n in range(4):
                b = 2 * (n % 2)
                pe.wait(t_w, bank_free[b], bank_free[b + 1], t_u)
                for k in range(8):
                    mm(ps[:, b, :], wv[:, k, n * 128:n * 128 + 128],
                       uT[:, k * T_ALL + 256:(k + 1) * T_ALL], k == 0, k == 7)
                    t = (mmt if k == 7 else mm)(ps[:, b + 1, 0:256], wv[:, k, n * 128:n * 128 + 128],
                                                uT[:, k * T_ALL:k * T_ALL + 256], k == 0, k == 7)
                    if k == 3:
                        yield
                r = raw[n % 2]
                if n < 2:
                    z = [prev.get("slots")]
                    pool.do(lambda e, r=r: e.memset(r[:, 0:2], 0.0), z)
                    pool.do(lambda e, r=r: e.memset(r[:, 258:260], 0.0))
                    t_pad = pool.do(lambda e, r=r: e.memset(r[:, 772:774], 0.0))
                acopy(r[:, 260:772], ps[:, b, :], t, prev.get(("raw", n % 2)), prev.get("slots"))
                t = acopy(r[:, 2:258], ps[:, b + 1, 0:256])
                bank_free[b] = bank_free[b + 1] = t
                tile_ = 4 * j + n
                cw = V("conv", 5 * tile_, 5 * tile_ + 5)
                vts(cv[n], r[:, 0:770], cw[:, 0:1], None, MUL, None, t, t_pad, prev.get("cv"))
                for q in range(1, 5):
                    t = vstt(cv[n], r[:, q:q + 770], cw[:, q:q + 1], cv[n], MUL, ADD)
                prev[("raw", n % 2)] = t
                t_c.append(t)
                yield
            ring_free[i] = bank_free[2]
            i, w, t_w = wload(D["w_z"][j])
            wv = w[:, 0:2048].rearrange("p (k m) -> p k m", k=8)
            t_zs = []
            for c in range(6):
                b = c // 2
                if c % 2 == 0:
                    pe.wait(t_w, bank_free[b])
                for k in range(8):
                    t = (mmt if k == 7 else mm)(ps[:, b, (c % 2) * 256:(c % 2) * 256 + 256],
                                                uT[:, k * T_ALL + c * 128:k * T_ALL + c * 128 + 128],
                                                wv[:, k, :], k == 0, k == 7)
                t_zs.append(t)
                yield
            ring_free[i] = t
            dst = [qT[par], kT[par], None, None]
            t_s = []
            for n in range(4):
                o = dst[n] if n < 2 else cv[n][:, 0:T_ALL]
                if n < 2:
                    aact(o[:, 0:256], cv[n][:, 0:256], ACT.Silu, t_c[n], prev.get(("qk", par)))
                    t_s.append(aact(o[:, 256:768], cv[n][:, 258:770], ACT.Silu))
                else:
                    aact(cv[n][:, 0:256], cv[n][:, 0:256], ACT.Silu, t_c[n])
                    t_s.append(aact(cv[n][:, 258:770], cv[n][:, 258:770], ACT.Silu))
            for b in range(3):
                bank_free[b] = aact(zg[:, b * 512:b * 512 + 512], ps[:, b, :], ACT.Silu, t_zs[2 * b + 1],
                                    prev.get(("zg", par)))
            table(LN_SET)
            t_z = pool.do(lambda e: e.tensor_tensor(
                zg.rearrange("p (c n) -> p c n", n=128), zg.rearrange("p (c n) -> p c n", n=128),
                bc(onorm, 1, [128, 12, 128]), MUL), bank_free[2], t_on)
            yield
            t_qk = []
            for n in range(2):
                x = dst[n]
                t = vtt(sqA, x, x, MUL, t_s[n], prev.get("sqA"))
                pe.wait(t, bank_free[2], bank_free[3])
                mm(ps[:, 2, :], ones, sqA[:, 0:512], True, True)
                t = mmt(ps[:, 3, 0:256], ones, sqA[:, 512:768], True, True)
                prev["sqA"] = t
                yield
                t = aact(rsA, psf[:, 1024:1024 + T_ALL], ACT.Ln, t, prev.get("rsA"), bias=eps)
                bank_free[2] = bank_free[3] = t
                if n == 0:
                    t = aact(rsA, rsA, ACT.Exp, scale=-0.5, bias=K("lnq"))
                else:
                    t = aact(rsA, rsA, ACT.Exp, scale=-0.5)
                t = vtt(x, x, rsA, MUL, t)
                prev["rsA"] = t
                t_qk.append(t)
                yield
            pe.wait(t_qk[1], bank_free[0], bank_free[1], prev.get(("kN", par)))
            for c in range(6):
                t = (trt if c == 5 else tr)(ps[:, c // 4, (c % 4) * 128:(c % 4) * 128 + 128],
                                            kT[par][:, c * 128:c * 128 + 128])
            t = acopy(kN[par], psf[:, 0:T_ALL], t, prev.get(("kN", par)))
            bank_free[0] = bank_free[1] = t
            t_k = t
            yield
            vv = vN[par].rearrange("p (c h e) -> p c h e", c=6, h=2)
            t_v = []
            for h in range(2):
                src = cv[2 + h]
                b = 2 if h == 0 else 0
                pe.wait(t_s[2 + h], bank_free[b], bank_free[b + 1])
                for c in range(6):
                    a = c * 128 + (2 if c >= 2 else 0)
                    t = (trt if c == 5 else tr)(ps[:, b + c // 4, (c % 4) * 128:(c % 4) * 128 + 128],
                                                src[:, a:a + 128])
                t = vcopy(vv[:, :, h, :], psf[:, b * 512:b * 512 + T_ALL].rearrange("p (c e) -> p c e", c=6),
                          t, prev.get(("vN", par)))
                bank_free[b] = bank_free[b + 1] = t
                t_v.append(t)
                yield
            prev["cv"] = t_v[1]
            prev["p_done"] = [t_v[1], t_k, t_z]
            return_[0] = (t_qk, t_k, t_v, t_z)

        return_ = [None]

        def invert(j, c, slot, made, out):
            par = j % 2
            t_qk = made[0]
            T1, KB, AT, Y, X = slots[slot]
            NB, Q = KB, T1
            b0, b1 = 2 + 2 * slot, 3 + 2 * slot
            h0 = 2 * j
            gsl = gt.rearrange("p (c d h) -> p c d h", c=6, d=2)[:, c, :, h0:h0 + 2]
            t = pool.do(lambda e: e.tensor_tensor(
                u4(X), bc(K("strict").rearrange("p (d s) -> p d s", d=2), 2, [128, 2, 2, 128]),
                bc(gsl, 3, [128, 2, 2, 128]), MUL), t_g, prev.get("p_done"), prev.get(("slot", slot)))
            pe.wait(t, bank_free[b0])
            for u in range(4):
                t = (mmt if u == 3 else mm)(ps[:, b0, u * 128:u * 128 + 128], X[:, u * 128:u * 128 + 128],
                                            K("tri", (u // 2) * 128, (u // 2) * 128 + 128), True, True)
            t_e = aact(T1, ps[:, b0, :], ACT.Exp, t, prev.get("p_done"), prev.get(("slot", slot)))
            yield
            kc, qc = kT[par][:, c * 128:c * 128 + 128], qT[par][:, c * 128:c * 128 + 128]
            pe.wait(t_qk, bank_free[b1])
            mm(ps[:, b1, 0:128], kc, kc, True, True)
            t = mmt(ps[:, b1, 128:256], kc, qc, True, True)
            for u in range(4):
                bcol = cols(beta, c, u // 2, h0 + u % 2, 1)
                t_kb = acopy(KB[:, u * 128:u * 128 + 128], ps[:, b1, 0:128], t, t_small, scale=bcol)
            vtt(u4(T1), u4(T1), bc(K("tri").rearrange("p (d s) -> p d s", d=2), 2, [128, 2, 2, 128]), MUL, t_e)
            t_at = vtt(AT, T1, KB, MUL, t_kb)
            o = PT[:, c * 512:c * 512 + 512].rearrange("p (u s) -> p u s", u=4)
            t_pt = vtt(o, T1.rearrange("p (u s) -> p u s", u=4), bc(ps[:, b1, 128:256], 1, [128, 4, 128]),
                       MUL, prev.get("Yf"))
            bank_free[b1] = t_pt
            yield

            def blocks(lv, *toks):
                m = K("mask", lv * 256, lv * 256 + 256).rearrange("p (d s) -> p d s", d=2)
                return pool.do(lambda e: e.tensor_tensor(u4(NB), u4(AT), bc(m, 2, [128, 2, 2, 128]), MUL),
                               *toks)

            def un(x, u):
                return x[:, u * 128:u * 128 + 128]

            identB = bc(ident, 1, [128, 4, 128])

            def v4(x):
                return x.rearrange("p (u s) -> p u s", u=4)

            t = blocks(0, t_at)
            t_y = vtt(v4(Y), v4(NB), identB, ADD, t)
            t_nb = blocks(1, t_y)
            t_x = None
            for lv in range(1, 7):
                pe.wait(t_y, bank_free[b0])
                for u in range(4):
                    t = (trt if u == 3 else tr)(ps[:, b0, u * 128:u * 128 + 128], un(Y, u))
                t_x = acopy(X, ps[:, b0, :], t)
                bank_free[b0] = t_x
                yield
                pe.wait(t_x, t_nb, bank_free[b1])
                for u in range(4):
                    t = (mmt if u == 3 else mm)(ps[:, b1, u * 128:u * 128 + 128], un(NB, u), un(X, u),
                                                True, True)
                t_p = t
                t_q = vtt(v4(Q), ps[:, b1, :].rearrange("p (u s) -> p u s", u=4), identB, ADD, t_p)
                bank_free[b1] = t_q
                if lv < 6:
                    t_nb = blocks(lv + 1, t_p)
                yield
                pe.wait(t_q, bank_free[b0])
                for u in range(4):
                    t = (mmt if u == 3 else mm)(ps[:, b0, u * 128:u * 128 + 128], un(Q, u), un(Y, u),
                                                True, True)
                t_y = acopy(Y if lv < 6 else Yf[:, c * 512:c * 512 + 512], ps[:, b0, :], t,
                            prev.get("Yf") if lv == 6 else None)
                bank_free[b0] = t_y
                yield
            prev[("slot", slot)] = [t_y, t]
            out[c] = [t_y, t_pt]

        def scan(j, made, inv):
            par, zg = j % 2, zgs[j % 2]
            t_qk, t_k, t_v, t_z = made
            h0 = 2 * j
            t_S = pool.do(lambda e: e.memset(S, 0.0), prev.get("S"))
            vv = vN[par].rearrange("p (c h e) -> p c h e", c=6, h=2)
            order = list(zip([0, 1, 2, 3, 4, 5], [1, 0, 5, 4, 3, 2]))
            t_vd = t_su = None
            for step, cc in enumerate(order):
                pe.wait(t_S, t_qk, bank_free[4], bank_free[5], inv[cc[0]], inv[cc[1]])
                for d in range(2):
                    c = cc[d]
                    t = (mmt if d else mm)(ps[:, 4, d * 256:d * 256 + 256], kT[par][:, c * 128:c * 128 + 128],
                                           S[:, d * 256:d * 256 + 256], True, True)
                t_ks = t
                for d in range(2):
                    c = cc[d]
                    t = (mmt if d else mm)(ps[:, 5, d * 256:d * 256 + 256], qT[par][:, c * 128:c * 128 + 128],
                                           S[:, d * 256:d * 256 + 256], True, True)
                t_qs = t
                for u in range(4):
                    c = cc[u // 2]
                    t = vstt(rr[:, u * 128:u * 128 + 128], ps[:, 4, u * 128:u * 128 + 128],
                             cols(neg_eg, c, u // 2, h0 + u % 2, 1), vv[:, c, u % 2, :], MUL, ADD,
                             t_ks, t_v, t_small)
                t_r = bank_free[4] = t
                for u in range(4):
                    c = cc[u // 2]
                    t = acopy(qs[:, u * 128:u * 128 + 128], ps[:, 5, u * 128:u * 128 + 128], t_qs,
                              prev.get("qs"), scale=cols(eg, c, u // 2, h0 + u % 2, 1))
                t_q = bank_free[5] = t
                yield
                pe.wait(t_r, bank_free[6])
                for u in range(4):
                    c = cc[u // 2]
                    t = (mmt if u == 3 else mm)(ps[:, 6, u * 128:u * 128 + 128],
                                                Yf[:, c * 512 + u * 128:c * 512 + u * 128 + 128],
                                                rr[:, u * 128:u * 128 + 128], True, True)
                for d in range(2):
                    x = vn.rearrange("p (d h e) -> p d h e", d=2, h=2)[:, d]
                    t_vn = vtt(x, ps[:, 6, d * 256:d * 256 + 256].rearrange("p (h e) -> p h e", h=2),
                               bc(cols(beta, cc[d], d, h0), 2, [128, 2, 128]), MUL, t, prev.get("vn"))
                bank_free[6] = t_vn
                for d in range(2):
                    x = vd.rearrange("p (d h e) -> p d h e", d=2, h=2)[:, d]
                    y = vn.rearrange("p (d h e) -> p d h e", d=2, h=2)[:, d]
                    t_vd = vtt(x, y, bc(cols(kdec, cc[d], d, h0), 2, [128, 2, 128]), MUL, prev.get("vd"))
                yield
                pe.wait(t_vd, t_k, bank_free[7])
                for d in range(2):
                    c = cc[d]
                    t = (mmt if d else mm)(ps[:, 7, d * 256:d * 256 + 256], kN[par][:, c * 128:c * 128 + 128],
                                           vd[:, d * 256:d * 256 + 256], True, True)
                t_su = prev["vd"] = t
                pe.wait(t_vn, bank_free[6])
                for u in range(4):
                    c = cc[u // 2]
                    t = (mmt if u == 3 else mm)(ps[:, 6, u * 128:u * 128 + 128],
                                                PT[:, c * 512 + u * 128:c * 512 + u * 128 + 128],
                                                vn[:, u * 128:u * 128 + 128], True, True)
                t_o = prev["vn"] = t
                for u in range(4):
                    c = cc[u // 2]
                    x = S[:, u * 128:u * 128 + 128]
                    t_S = vstt(x, x, cols(gl, c, u // 2, h0 + u % 2, 1), ps[:, 7, u * 128:u * 128 + 128],
                               MUL, ADD, t_su)
                bank_free[7] = t_S
                vtt(oF[:, cc[0] * 256:cc[0] * 256 + 256], ps[:, 6, 0:256], qs[:, 0:256], ADD, t_o, t_q,
                    prev.get("oF"))
                t = vtt(oB[:, cc[1] * 256:cc[1] * 256 + 256], ps[:, 6, 256:512], qs[:, 256:512], ADD)
                bank_free[6] = prev["qs"] = t
                yield
            prev["S"] = [t_S, t_su]
            prev[("qk", par)] = prev[("kN", par)] = prev[("vN", par)] = [t_su, t_r, t_qs]
            prev["Yf"] = [t_o]
            t_sum = t
            t = vtt(oF, oF, oB, ADD)
            t = aact(oB, oF, ACT.Square, t)
            o3 = oF.rearrange("p (c e) -> p c e", e=128)
            t = dve.do(lambda e: e.tensor_reduce(rr[:, 0:12], oB.rearrange("p (c e) -> p c e", e=128), AX, ADD),
                       t)
            aact(rr[:, 0:12], rr[:, 0:12], ACT.Ln, t, bias=eps, scale=1.0 / 128)
            t = aact(rr[:, 0:12], rr[:, 0:12], ACT.Exp, scale=-0.5)
            yield
            vtt(o3, o3, bc(rr[:, 0:12], 2, [128, 12, 128]), MUL, t)
            t = vtt(oF, oF, zg, MUL, t_z)
            prev[("zg", par)] = t
            pe.wait(t, bank_free[4], bank_free[5], bank_free[6])
            for h in range(2):
                for c in range(6):
                    n = h * 6 + c
                    t = (trt if n == 11 else tr)(ps[:, 4 + n // 4, (n % 4) * 128:(n % 4) * 128 + 128],
                                                 oF[:, c * 256 + h * 128:c * 256 + h * 128 + 128])
            prev["oF"] = t
            yield
            t = acopy(oB[:, 0:1536], psf[:, 2048:2048 + 1536], t)
            bank_free[4] = bank_free[5] = bank_free[6] = t
            s_y[0] = act.dma(sem_y, D["scratch"][j], oB, t)
            prev["oF"] = [prev["oF"], s_y[0]]

        sem_y, s_y = dsem("s_y"), [None]

        def run(*gens):
            gens = list(gens)
            while gens:
                for g in list(gens):
                    try:
                        next(g)
                    except StopIteration:
                        gens.remove(g)

        run(project(0))
        made = return_[0]
        for j in range(8):
            inv = {}
            for wave in range(2):
                run(*[invert(j, 3 * wave + s, s, made, inv) for s in range(3)])
            prev["slots"] = [prev[("slot", s)] for s in range(3)]
            if j < 7:
                run(scan(j, made, inv), project(j + 1))
                made = return_[0]
            else:
                run(scan(j, made, inv))

        def everything():
            return [q.last for q in (pe, dve, act, pool) if q.last is not None]

        top[0] = mark_0
        start = everything() + [s_y[0], t_on]
        ring.append(take(SLOT))
        ring_sem.append(dsem("ring2"))
        ring_free.append(start)
        hT = take(8 * T_ALL)
        mark_b = top[0]
        yT = take(16 * T_ALL)
        t_h = sp.dma(s_h, hT, D["xT"], start)
        t_y = act.dma(sem_y, yT.rearrange("p (j n) -> p j n", j=8), D["scratch"].rearrange("j p n -> p j n"),
                      start)

        def out_product(slabs, tiles_in_slab, nk, src, width, use, ready, first=0):
            n = 0
            for parts in slabs:
                i, w, t_w = wload(*parts)
                m = tiles_in_slab
                for x in range(m):
                    b = first + 2 * (n % 2) if width > 512 else first + n % 4
                    pe.wait(t_w, ready, bank_free[b], bank_free[b + 1] if width > 512 else None)
                    for k in range(nk):
                        lhsT = w[:, (k * m + x) * 128:(k * m + x) * 128 + 128]
                        if width > 512:
                            s = src(k)
                            mm(ps[:, b, :], lhsT, s[:, 256:768], k == 0, k == nk - 1)
                            t = (mmt if k == nk - 1 else mm)(ps[:, b + 1, 0:256], lhsT, s[:, 0:256],
                                                             k == 0, k == nk - 1)
                        else:
                            t = (mmt if k == nk - 1 else mm)(ps[:, b, 0:width], lhsT, src(k),
                                                             k == 0, k == nk - 1)
                    r = use(n, b, t)
                    bank_free[b] = r
                    if width > 512:
                        bank_free[b + 1] = r
                    n += 1
                ring_free[i] = t
            return r

        def add_gated(layer, width):
            def use(n, b, t):
                o = hT[:, n * T_ALL:(n + 1) * T_ALL]
                r = vstt(o[:, 256:768], ps[:, b, :], modv(layer, 16 + n, 0), o[:, 256:768], MUL, ADD, t, t_h)
                if width > 512:
                    r = vstt(o[:, 0:256], ps[:, b + 1, 0:256], modv(layer, 16 + n, 1), o[:, 0:256], MUL, ADD)
                return r
            return use

        t_h = out_product([[D["dn_out"][n]] for n in range(4)], 2, 16, lambda k: yT[:, k * T_ALL:(k + 1) * T_ALL],
                          T_ALL, add_gated(0, T_ALL), t_y)

        top[0] = mark_b
        uT = take(8 * T_ALL)
        mark_c = top[0]
        rstd = take(T_ALL)
        sq = [take(T_ALL), take(T_ALL)]
        t_u = modulate_again = None
        bank_free[3] = bank_free[4] = everything()
        t_mod[1] = [t_mod[1]] + everything()
        t_u = modulate(1, uT)
        top[0] = mark_c
        start = everything()
        qT4 = take(8 * 512)
        zT = take(8 * 512)
        kT2 = take(2 * T_ALL)
        vN2 = take(6 * 256)
        ax = take(1024)
        t_ax = act.dma(s_small, ax, D["axial"], start)
        sqb, rsb = take(T_ALL), take(T_ALL)
        t_sq = t_rs = None

        def rope(x, perm, cos, sin, b, ready, p0=0, p1=128):
            np_ = 128 if p1 == 128 else 96
            pe.wait(ready, bank_free[b])
            t = mmt(ps[0:np_, b, :], perm, x[0:np_], True, True)
            t = vtt(sqb[p0:p1, 0:512], ps[p0:p1, b, :], sin, MUL, t, t_ax, everything())
            bank_free[b] = t
            vtt(x[p0:p1], x[p0:p1], cos, MUL)
            return vtt(x[p0:p1], x[p0:p1], sqb[p0:p1, 0:512], ADD)

        def norm_fm(x, width, g, b, ready, div=128.0):
            t = aact(sqb[:, 0:width], x, ACT.Square, ready, everything())
            pe.wait(t, bank_free[b], bank_free[b + 1])
            t = mmt(ps[:, b, :], ones, sqb[:, 0:512], True, True)
            if width > 512:
                t = mmt(ps[:, b + 1, 0:width - 512], ones, sqb[:, 512:width], True, True)
            t = aact(rsb[:, 0:width], psf[:, b * 512:b * 512 + width], ACT.Ln, t, bias=eps, scale=1.0 / div)
            bank_free[b] = bank_free[b + 1] = t
            t = aact(rsb[:, 0:width], rsb[:, 0:width], ACT.Exp, scale=-0.5)
            return vstt(x, x, g, rsb[:, 0:width], MUL, MUL, t)

        def lat(k):
            return uT[:, k * T_ALL + 256:(k + 1) * T_ALL]

        t_q = [None] * 8

        def use_q(n, b, t):
            x = qT4[:, n * 512:(n + 1) * 512]
            r = acopy(x, ps[:, b, :], t, start)
            t_q[n] = norm_fm(x, 512, V("qn_g"), 4, r)
            t_q[n] = rope(x, K("perm"), ax[:, 0:512], ax[:, 512:1024], 6, t_q[n])
            return r

        out_product([[D["att_in"][n]] for n in range(2)], 4, 8, lat, 512, use_q, t_u)
        i, w, t_w = wload(D["att_in"][2])
        wv = w.rearrange("p (k m) -> p k m", k=8)
        for n in range(2):
            pe.wait(t_w, bank_free[2 * n], bank_free[2 * n + 1])
            for k in range(8):
                mm(ps[:, 2 * n, :], wv[:, k, n * 128:n * 128 + 128], lat(k), k == 0, k == 7)
                t = (mmt if k == 7 else mm)(ps[:, 2 * n + 1, 0:256], wv[:, k, n * 128:n * 128 + 128],
                                            uT[:, k * T_ALL:k * T_ALL + 256], k == 0, k == 7)
            x = kT2[:, n * T_ALL:(n + 1) * T_ALL]
            acopy(x[:, 256:768], ps[:, 2 * n, :], t, start)
            t = acopy(x[:, 0:256], ps[:, 2 * n + 1, 0:256], t)
            bank_free[2 * n] = bank_free[2 * n + 1] = t
            t = norm_fm(x, T_ALL, V("kn_g"), 4, t)
            t_k = rope(x[:, 256:768], K("perm"), ax[:, 0:512], ax[:, 512:1024], 6, t)
        for c in range(6):
            pe.wait(bank_free[c % 4])
            for k in range(8):
                t = (mmt if k == 7 else mm)(ps[:, c % 4, 0:256], uT[:, k * T_ALL + c * 128:k * T_ALL + c * 128 + 128],
                                            wv[:, k, 256:512], k == 0, k == 7)
            t_v = bank_free[c % 4] = acopy(vN2[:, c * 256:c * 256 + 256], ps[:, c % 4, 0:256], t)
        ring_free[i] = t

        def use_z(n, b, t):
            return aact(zT[:, n * 512:(n + 1) * 512], ps[:, b, :], ACT.Silu, t, start)

        t_z = out_product([[D["att_in"][n]] for n in (3, 4)], 4, 8, lat, 512, use_z, t_u)
        table(LN_SET)
        top[0] = top[0] - 2 * T_ALL
        start = everything()

        PL = [take(T_ALL) for _ in range(3)]
        small = take(3 * 8)
        PTs = [take(6 * 512) for _ in range(2)]
        t_pt = {0: start, 1: start}
        lane_last = [start, start, start]

        def rows(lane, width, scores, ready, scale, dst, bias=None, keep=None):
            b = 2 * lane
            P = PL[lane][:, 0:width]
            sm = small[:, lane * 8:lane * 8 + 8]
            nm, den = sm[:, 1:2], sm[:, 2:3]
            if keep is not None:
                nm, den = keep
            pe.wait(ready, bank_free[b], bank_free[b + 1])
            t = scores(b)
            src = psf[:, b * 512:b * 512 + width]
            if bias is not None:
                vstt(P, src, scale, bias, MUL, ADD, t, lane_last[lane])
                src, es = P, 1.0
            else:
                es = scale
            dve.do(lambda e, o=sm[:, 0:1], s=src: e.reduce_max(o, s, AX), t, lane_last[lane])
            t = vts(nm, sm[:, 0:1], -es, None, MUL, None)
            t = aact(P, src, ACT.Exp, t, lane_last[lane], bias=nm, scale=es, accum=den)
            bank_free[b] = bank_free[b + 1] = t
            yield
            dve.do(lambda e, o=sm[:, 3:4], s=den: e.reciprocal(o, s), t)
            t = vts(P, P, sm[:, 3:4], None, MUL, None)
            nk = width // 128
            pe.wait(t, bank_free[b])
            for c in range(nk):
                t = (trt if c == nk - 1 else tr)(psf[:, b * 512 + c * 128:b * 512 + c * 128 + 128],
                                                 P[:, c * 128:c * 128 + 128])
            out, toks = dst()
            t = acopy(out, psf[:, b * 512:b * 512 + width].rearrange("p (c q) -> p c q", q=128), t, toks)
            bank_free[b] = bank_free[b + 1] = lane_last[lane] = t
            done[0] = t
            yield

        done = [None]

        def lanes(units):
            at, live, free = 0, [], [0, 1, 2]
            pending = []
            while at < len(units) or live or pending:
                while free and at < len(units) and not (pending and len(pending) > 1):
                    kind, f = units[at]
                    at += 1
                    if kind == "f":
                        pending.append((f, [u for u in live]))
                        continue
                    lane = free.pop(0)
                    live.append([lane, f(lane)])
                for u in list(live):
                    try:
                        next(u[1])
                    except StopIteration:
                        live.remove(u)
                        free.append(u[0])
                while pending and not any(any(u is x for x in live) for u in pending[0][1]):
                    pending.pop(0)[0]()

        units = []
        t_yv = [None]
        for h in range(8):
            kv = h // 4
            PTh = PTs[h % 2].rearrange("p (c q) -> p c q", c=6)
            toks = {}
            for q4 in range(4):
                def unit(lane, h=h, kv=kv, q4=q4, PTh=PTh, toks=toks):
                    def scores(b):
                        q = qT4[:, h * 512 + q4 * 128:h * 512 + q4 * 128 + 128]
                        mm(ps[:, b, :], q, kT2[:, kv * T_ALL:kv * T_ALL + 512], True, True)
                        return mmt(ps[:, b + 1, 0:256], q, kT2[:, kv * T_ALL + 512:kv * T_ALL + 768], True, True)

                    def go():
                        yield from rows(lane, T_ALL, scores, [t_q[h], t_k], 128.0 ** -0.5,
                                        lambda: (PTh[:, :, q4 * 128:q4 * 128 + 128], t_pt[h % 2]))
                        toks[q4] = done[0]
                    return go()
                units.append(("u", unit))

            def pv(h=h, kv=kv, PTh=PTh, toks=toks):
                b = 6 + h % 2
                pe.wait(list(toks.values()), t_v, bank_free[b])
                for c in range(6):
                    t = (mmt if c == 5 else mm)(ps[:, b, :], vN2[:, c * 256 + kv * 128:c * 256 + kv * 128 + 128],
                                                PTh[:, c, :], c == 0, c == 5)
                t_pt[h % 2] = t
                z = zT[:, h * 512:(h + 1) * 512]
                bank_free[b] = t_yv[0] = vtt(z, ps[:, b, :], z, MUL, t, t_z)
            units.append(("f", pv))
        lanes(units)

        t_h = out_product([[D["att_out"][n]] for n in range(2)], 4, 8, lambda k: zT[:, k * 512:(k + 1) * 512],
                          512, add_gated(1, 512), t_yv[0])
        top[0] = mark_b
        start = everything()
        X = take(8 * 512)
        hn = take(8 * 512)
        r5, sq5 = take(512), [take(512), take(512)]
        t_r, _ = mean_square(lambda k: hT[:, k * T_ALL + 256:(k + 1) * T_ALL], 8, 512, 4, sq5, [t_h] + start,
                             r5, bank_free[4], 1024.0)
        for k in range(8):
            t_x = vstt(X[:, k * 512:(k + 1) * 512], hT[:, k * T_ALL + 256:(k + 1) * T_ALL], V("final_g", k, k + 1),
                       r5, MUL, MUL, t_r, start)

        start = everything()
        s_c = dsem("s_c")

        def norm_to(out, src, n, g, div, ready):
            t, _ = mean_square(lambda k: src[:, k * 512:(k + 1) * 512], n, 512, 4, sq5,
                               [ready] + everything(), r5, bank_free[4], div)
            bank_free[4] = everything()
            for k in range(n):
                t2 = vstt(out[:, k * 512:(k + 1) * 512], src[:, k * 512:(k + 1) * 512], g[:, k:k + 1], r5,
                          MUL, MUL, t)
            return t2

        t_hn = norm_to(hn, X, 8, V("pre_mix"), 1024.0, t_x)

        def hk(k):
            return hn[:, k * 512:(k + 1) * 512]

        y_mla, y_dil, y_mem = (hT[:, n * 2048:(n + 1) * 2048] for n in range(3))
        mark_d = top[0]

        cosT, sinT = take(512), take(512)
        mark_cs = top[0]
        posi, pos, ang, rn, rr2 = (take(512) for _ in range(5))
        t_p = act.dma(s_c, posi[0:96].bitcast(I32), D["positions"].partition_broadcast(96), everything())
        vcopy(pos[0:96], posi[0:96].bitcast(I32), t_p, everything())
        P96 = slice(0, 96)
        vts(ang[P96], pos[P96], cst[0:96, CONST["invf"][0]:CONST["invf"][1]], None, MUL, None)
        TWO_PI = 2.0 * math.pi
        MAGIC = 12582912.0
        C1 = 6.28125
        C2 = float((np.array(TWO_PI - C1, np.float32).view(np.int32) & np.int32(-4096)).view(np.float32))
        C3 = TWO_PI - C1 - C2
        vts(rn[P96], ang[P96], 1.0 / TWO_PI, None, MUL, None)
        vts(rn[P96], rn[P96], MAGIC, None, ADD, None)
        vts(rn[P96], rn[P96], -MAGIC, None, ADD, None)
        for c_ in (C1, C2, C3):
            vstt(ang[P96], rn[P96], -c_, ang[P96], MUL, ADD)
        PI = 3.1415925
        t = vts(rr2[P96], ang[P96], PI, -PI, ALU.min, ALU.max)
        t_s = aact(sinT[P96], rr2[P96], ACT.Sin, t, everything())
        vts(ang[P96], ang[P96], math.pi / 2, None, ADD, None)
        vts(rn[P96], ang[P96], math.pi, -TWO_PI, ALU.is_gt, MUL)
        vtt(ang[P96], ang[P96], rn[P96], ADD)
        t = vts(ang[P96], ang[P96], PI, -PI, ALU.min, ALU.max)
        t_cs = aact(cosT[P96], ang[P96], ACT.Sin, t)
        table(LN_SET)
        top[0] = mark_cs
        start = everything()

        wide = take(512)
        t_wide = act.dma(s_c, wide, D["bias"][:, 2048:2560], start)
        sqb = take(512)
        cq, ckv = take(3 * 512), take(2 * 512)
        qm, km = take(8 * 512), take(8 * 512)
        vm = take(4 * 512)
        mark_e = top[0]
        wkr = take(8 * 96)
        kr = take(512)
        t = pool.do(lambda e: e.memset(wkr, 0.0), start)
        t_wk = act.dma(s_c, wkr.rearrange("p (k m) -> p k m", k=8)[:, :, 64:96],
                       D["w_kr"].rearrange("p (k m) -> p k m", k=8), t)

        def into(buf, func=None):
            def use(n, b, t):
                return acopy(buf[:, n * 512:(n + 1) * 512], ps[:, b, :], t, start)
            return use

        t = out_product([[D["w_cq"]]], 3, 8, hk, 512, into(cq), t_hn)
        t_cq = norm_to(cq, cq, 3, V("mla_q"), 384.0, t)
        t = out_product([[D["w_ckv"]]], 2, 8, hk, 512, into(ckv), t_hn)
        t_ckv = norm_to(ckv, ckv, 2, V("mla_kv"), 256.0, t)
        pe.wait(t_wk, bank_free[5])
        for k in range(8):
            t = (mmt if k == 7 else mm)(ps[0:96, 5, :], wkr[:, k * 96:k * 96 + 96], hk(k), k == 0, k == 7)
        t = acopy(kr[0:96], ps[0:96, 5, :], t, start)
        bank_free[5] = t
        perm96 = cst[0:96, CONST["perm96"][0]:CONST["perm96"][1]]
        t_kr = rope(kr, perm96, cosT[64:96], sinT[64:96], 5, t, 64, 96)
        for h in range(8):
            t_kk = pool.do(lambda e, h=h: e.tensor_copy(km[64:96, h * 512:h * 512 + 512], kr[64:96]), t_kr, start)
        i, w, t_w = wload(D["w_uq"])
        t_qh = []
        for h in range(8):
            b = h % 4
            pe.wait(t_w, t_cq, bank_free[b])
            for k in range(3):
                t = (mmt if k == 2 else mm)(ps[0:96, b, :], w[:, k * 768 + h * 96:k * 768 + h * 96 + 96],
                                            cq[:, k * 512:(k + 1) * 512], k == 0, k == 2)
            x = qm[:, h * 512:(h + 1) * 512]
            t = bank_free[b] = acopy(x[0:96], ps[0:96, b, :], t, start)
            t_qh.append(rope(x, perm96, cosT[64:96], sinT[64:96], 5 + h % 2, t, 64, 96))
        ring_free[i] = [pe.last]
        i, w, t_w = wload(D["w_uk"], D["w_uv"])
        t_kh = []
        for h in range(0, 8, 2):
            b = (h // 2) % 4
            pe.wait(t_w, t_ckv, bank_free[b])
            for k in range(2):
                t = (mmt if k == 1 else mm)(ps[:, b, :], w[:, k * 512 + h * 64:k * 512 + h * 64 + 128],
                                            ckv[:, k * 512:(k + 1) * 512], k == 0, k == 1)
            acopy(km[0:64, h * 512:(h + 1) * 512], ps[0:64, b, :], t, start)
            t = bank_free[b] = acopy(km[0:64, (h + 1) * 512:(h + 2) * 512], ps[64:128, b, :], t)
            t_kh.append(t)
        for c in range(4):
            pe.wait(bank_free[c])
            for k in range(2):
                t = (mmt if k == 1 else mm)(ps[:, c, :], ckv[:, k * 512 + c * 128:k * 512 + c * 128 + 128],
                                            w[:, 1024 + k * 512:1024 + (k + 1) * 512], k == 0, k == 1)
            t_vm = bank_free[c] = acopy(vm[:, c * 512:(c + 1) * 512], ps[:, c, :], t, start)
        ring_free[i] = t

        def lane_buffers(width, pt):
            nonlocal_["PL"] = None
            start = everything()
            PL[:] = [take(width) for _ in range(3)]
            PTs[:] = [take(pt) for _ in range(2)]
            t_pt[0] = t_pt[1] = start
            lane_last[:] = [start] * 3

        nonlocal_ = {}
        small = take(3 * 8)
        top[0] = mark_e
        small = take(3 * 8)
        lane_buffers(512, 4 * 512)
        units = []
        for h in range(8):
            PTh = PTs[h % 2].rearrange("p (c q) -> p c q", c=4)
            toks = {}
            for q4 in range(4):
                def unit(lane, h=h, q4=q4, PTh=PTh, toks=toks):
                    n = 128 * (q4 + 1)

                    def scores(b):
                        return mmt(ps[:, b, 0:n], qm[0:96, h * 512 + q4 * 128:h * 512 + q4 * 128 + 128],
                                   km[0:96, h * 512:h * 512 + n], True, True)

                    def go():
                        yield from rows(lane, n, scores, [t_qh[h], t_kh[h // 2], t_kk, t_wide], 96.0 ** -0.5,
                                        lambda: (PTh[:, 0:q4 + 1, q4 * 128:q4 * 128 + 128], t_pt[h % 2]),
                                        bias=wide[:, 512 - n:512])
                        toks[q4] = done[0]
                    return go()
                units.append(("u", unit))

            def pv(h=h, PTh=PTh, toks=toks):
                b, p = 6 + (h // 2) % 2, 64 * (h % 2)
                pe.wait(list(toks.values()), t_vm, bank_free[b])
                for c in range(4):
                    t = (mmt if c == 3 else mm)(ps[p:p + 64, b, c * 128:512],
                                                vm[:, c * 512 + h * 64:c * 512 + h * 64 + 64],
                                                PTh[:, c, c * 128:512], c == 0, c == 3)
                t_pt[h % 2] = t
                if h % 2:
                    bank_free[b] = t_ym[0] = vcopy(y_mla[:, (h // 2) * 512:(h // 2 + 1) * 512], ps[:, b, :], t)
            units.append(("f", pv))
        t_ym = [None]
        lanes(units)

        top[0] = mark_d
        start = everything()
        tab = take(2048)
        t_tab = act.dma(s_c, tab, D["bias"][:, 0:2048], start)
        O = take(12 * 512)
        NM, DEN, LSE = take(48), take(48), take(48)
        small = take(3 * 8)
        mark_f = top[0]
        qd, kd, vd2 = take(2048), take(2048), take(2048)
        lane_buffers(256, 2 * 512)

        def natural(x, g):
            if g == 0:
                return x.rearrange("p (r l) -> p r l", r=4)
            if g == 1:
                return x.rearrange("p (l r) -> p r l", r=4)
            return x.rearrange("p (l m f) -> p m f l", m=4, f=4)

        hp = take(8 * 512)
        for k in range(8):
            t_hp = pool.do(lambda e, k=k: e.tensor_copy(
                hp[:, k * 512:(k + 1) * 512].rearrange("p (m f l) -> p m f l", m=4, f=4), natural(hk(k), 2)),
                start, t_hn)
        for g in range(3):
            free_qkv = everything()
            t_dq = out_product([[D["w_dil"][g]]], 4, 8, hk, 512,
                               lambda n, b, t: acopy(qd[:, n * 512:(n + 1) * 512].rearrange("p (a c) -> p a c", a=4)
                                                     if g < 2 else
                                                     qd[:, n * 512:(n + 1) * 512].rearrange("p (m f l) -> p m f l",
                                                                                            m=4, f=4),
                                                     natural(ps[:, b, :], g), t, free_qkv), t_hn)
            t_dk = out_product([[D["w_dil"][3 + g]]], 4, 8, hk, 512,
                               lambda n, b, t: acopy(kd[:, n * 512:(n + 1) * 512].rearrange("p (a c) -> p a c", a=4)
                                                     if g < 2 else
                                                     kd[:, n * 512:(n + 1) * 512].rearrange("p (m f l) -> p m f l",
                                                                                            m=4, f=4),
                                                     natural(ps[:, b, :], g), t, free_qkv), t_hn)
            i, w, t_w = wload(D["w_dil"][6 + g])
            for c in range(4):
                pe.wait(t_w, bank_free[c], t_hp if g == 2 else None)
                for k in range(8):
                    hv = hp[:, k * 512 + c * 128:k * 512 + c * 128 + 128] if g == 2 else natural(hk(k), g)[:, c]
                    t = (mmt if k == 7 else mm)(ps[:, c, :], hv, w[:, k * 512:(k + 1) * 512],
                                                k == 0, k == 7)
                t_dv = bank_free[c] = acopy(vd2[:, c * 512:(c + 1) * 512], ps[:, c, :], t, free_qkv)
            ring_free[i] = t
            units = []
            for h in range(4):
                PTh = PTs[h % 2].rearrange("p (q c) -> p q c", c=256)
                toks = {}
                for q4 in range(4):
                    def unit(lane, h=h, q4=q4, PTh=PTh, toks=toks, g=g):
                        two = g == 0 and q4 > 0
                        n = 256 if two else 128
                        k0 = h * 512 + (q4 - two) * 128
                        if g == 0:
                            bias = tab[:, h * 256 + (0 if two else 128):h * 256 + 256]
                        else:
                            bias = tab[:, 512 + g * 512 + h * 128:512 + g * 512 + h * 128 + 128]
                        idx = g * 16 + h * 4 + q4

                        def scores(b):
                            return mmt(ps[:, b, 0:n], qd[:, h * 512 + q4 * 128:h * 512 + q4 * 128 + 128],
                                       kd[:, k0:k0 + n], True, True)

                        def go():
                            yield from rows(lane, n, scores, [t_dq, t_dk, t_tab], 128.0 ** -0.5,
                                            lambda: (PTh[:, q4, 0:n].rearrange("p (c q) -> p c q", q=128),
                                                     t_pt[h % 2]),
                                            bias=bias, keep=(NM[:, idx:idx + 1], DEN[:, idx:idx + 1]))
                            toks[q4] = done[0]
                        return go()
                    units.append(("u", unit))

                def pv(h=h, PTh=PTh, toks=toks, g=g):
                    b = 6 + h % 2
                    pe.wait(list(toks.values()), t_dv, bank_free[b])
                    for q4 in range(4):
                        two = g == 0 and q4 > 0
                        for c in range(1 + two):
                            vt = q4 - two + c
                            t = (mmt if (q4 == 3 and c == two) else mm)(
                                ps[:, b, q4 * 128:q4 * 128 + 128],
                                vd2[:, vt * 512 + h * 128:vt * 512 + h * 128 + 128],
                                PTh[:, q4, c * 128:c * 128 + 128], c == 0, c == two)
                    t_pt[h % 2] = t
                    o = O[:, (g * 4 + h) * 512:(g * 4 + h + 1) * 512]
                    p = ps[:, b, :].rearrange("p (a c) -> p a c", a=4) if g < 2 else \
                        ps[:, b, :].rearrange("p (m f l) -> p m f l", m=4, f=4)
                    bank_free[b] = t_oo[0] = vcopy(natural(o, g), p, t, start)
                units.append(("f", pv))
            t_oo = [None]
            lanes(units)
        top[0] = mark_f
        start = everything()
        LB = [take(512) for _ in range(3)]
        mx, sm5, tm5 = take(512), take(512), take(512)
        t = aact(LSE, DEN, ACT.Ln, start)
        t_lse = vtt(LSE, LSE, NM, SUB, t)
        for h in range(4):
            for g in range(3):
                b = g + 4 * (h % 2) if g + 4 * (h % 2) < 8 else 0
                pe.wait(t_lse, bank_free[b])
                for q4 in range(4):
                    idx = g * 16 + h * 4 + q4
                    t = (mmt if q4 == 3 else mm)(ps[:, b, q4 * 128:q4 * 128 + 128],
                                                 LSE[:, idx:idx + 1].to_broadcast([128, 128]), ident, True, True)
                p = ps[:, b, :].rearrange("p (a c) -> p a c", a=4) if g < 2 else \
                    ps[:, b, :].rearrange("p (m f l) -> p m f l", m=4, f=4)
                bank_free[b] = vcopy(natural(LB[g], g), p, t)
            vtt(mx, LB[0], LB[1], ALU.max)
            vtt(mx, mx, LB[2], ALU.max)
            for g in range(3):
                t = vtt(LB[g], LB[g], mx, SUB)
                t = aact(LB[g], LB[g], ACT.Exp, t)
                o = O[:, (g * 4 + h) * 512:(g * 4 + h + 1) * 512]
                if g == 0:
                    vcopy(sm5, LB[0], t)
                else:
                    vtt(sm5, sm5, LB[g], ADD, t)
                vtt(o, o, LB[g], MUL)
                if g:
                    vtt(O[:, h * 512:(h + 1) * 512], O[:, h * 512:(h + 1) * 512], o, ADD)
            t = aact(sm5, sm5, ACT.Ln, everything())
            t = aact(sm5, sm5, ACT.Exp, scale=-1.0)
            t_yd = vtt(y_dil[:, h * 512:(h + 1) * 512], O[:, h * 512:(h + 1) * 512], sm5, MUL, t)

        top[0] = mark_d
        start = everything()
        memT = take(8 * 256)
        t_m = act.dma(s_c, memT, D["memT"], start)
        small = take(3 * 8)
        qe, ke, ve = take(4 * 512), take(4 * 256), take(2 * 512)
        lane_buffers(256, 2 * 512)
        t_mq = out_product([[D["w_memq"]]], 4, 8, hk, 512, into(qe), t_hn)
        pe.wait(bank_free[4])
        tq = [None, None]
        for k in range(8):
            t = aact(sq5[k % 2][:, 0:256], memT[:, k * 256:(k + 1) * 256], ACT.Square, t_m, tq[k % 2], start)
            pe.wait(t)
            t = tq[k % 2] = mmt(ps[:, 4, 0:256], ones, sq5[k % 2][:, 0:256], k == 0, k == 7)
        t = aact(r5[:, 0:256], ps[:, 4, 0:256], ACT.Ln, t, bias=eps, scale=1.0 / 1024)
        bank_free[4] = t
        t = aact(r5[:, 0:256], r5[:, 0:256], ACT.Exp, scale=-0.5)
        for k in range(8):
            x = memT[:, k * 256:(k + 1) * 256]
            t_mn = vstt(x, x, V("g_mem", k, k + 1), r5[:, 0:256], MUL, MUL, t)

        def use_ke(n, b, t):
            return acopy(ke[:, n * 256:(n + 1) * 256], ps[:, b, 0:256], t)

        t_ke = out_product([[D["w_memkv"][0]]], 4, 8, lambda k: memT[:, k * 256:(k + 1) * 256], 256, use_ke, t_mn)
        i, w, t_w = wload(D["w_memkv"][1])
        for c in range(2):
            pe.wait(t_w, bank_free[c])
            for k in range(8):
                t = (mmt if k == 7 else mm)(ps[:, c, :], memT[:, k * 256 + c * 128:k * 256 + c * 128 + 128],
                                            w[:, k * 512:(k + 1) * 512], k == 0, k == 7)
            t_ve = bank_free[c] = acopy(ve[:, c * 512:(c + 1) * 512], ps[:, c, :], t)
        ring_free[i] = t
        units = []
        for h in range(4):
            PTh = PTs[h % 2].rearrange("p (c q) -> p c q", c=2)
            toks = {}
            for q4 in range(4):
                def unit(lane, h=h, q4=q4, PTh=PTh, toks=toks):
                    def scores(b):
                        return mmt(ps[:, b, 0:256], qe[:, h * 512 + q4 * 128:h * 512 + q4 * 128 + 128],
                                   ke[:, h * 256:(h + 1) * 256], True, True)

                    def go():
                        yield from rows(lane, 256, scores, [t_mq, t_ke], 128.0 ** -0.5,
                                        lambda: (PTh[:, :, q4 * 128:q4 * 128 + 128], t_pt[h % 2]))
                        toks[q4] = done[0]
                    return go()
                units.append(("u", unit))

            def pv(h=h, PTh=PTh, toks=toks):
                b = 6 + h % 2
                pe.wait(list(toks.values()), t_ve, bank_free[b])
                for c in range(2):
                    t = (mmt if c == 1 else mm)(ps[:, b, :], ve[:, c * 512 + h * 128:c * 512 + h * 128 + 128],
                                                PTh[:, c, :], c == 0, c == 1)
                t_pt[h % 2] = t
                bank_free[b] = t_ye[0] = vcopy(y_mem[:, h * 512:(h + 1) * 512], ps[:, b, :], t)
            units.append(("f", pv))
        t_ye = [None]
        lanes(units)

        top[0] = mark_d
        start = everything()
        M = take(8 * 512)
        gs = [take(512) for _ in range(2)]
        tp = [take(512) for _ in range(2)]
        t_tp = [start, start]
        n_ = 0
        for br, y in enumerate((y_mla, y_dil, y_mem)):
            i, w, t_w = wload(D["w_br"][br])
            for half in range(2):
                i2, w2, t_w2 = wload(D["w_gate"][2 * br + half])
                for x in range(4):
                    n = 4 * half + x
                    b = 2 * (n_ % 4)
                    pe.wait(t_w, t_w2, start, bank_free[b], bank_free[b + 1])
                    for k in range(8):
                        t = (mmt if k == 7 else mm)(ps[:, b, :], w2[:, k * 512 + x * 128:k * 512 + x * 128 + 128],
                                                    hk(k), k == 0, k == 7)
                    t_g2 = aact(gs[n_ % 2], ps[:, b, :], ACT.Sigmoid, t, t_tp[n_ % 2],
                                bias=V("b_gate", br * 8 + n, br * 8 + n + 1))
                    bank_free[b] = t_g2
                    for k in range(4):
                        t = (mmt if k == 3 else mm)(ps[:, b + 1, :],
                                                    w[:, k * 1024 + n * 128:k * 1024 + n * 128 + 128],
                                                    y[:, k * 512:(k + 1) * 512], k == 0, k == 3)
                    m = M[:, n * 512:(n + 1) * 512]
                    if br == 0:
                        t_M = bank_free[b + 1] = t_tp[n_ % 2] = vtt(m, ps[:, b + 1, :], gs[n_ % 2], MUL, t, t_g2, start)
                    else:
                        bank_free[b + 1] = vtt(tp[0], ps[:, b + 1, :], gs[n_ % 2], MUL, t, t_g2, start)
                        t_M = t_tp[n_ % 2] = vtt(m, m, tp[0], ADD)
                    n_ += 1
                ring_free[i2] = t
            ring_free[i] = t
        table(LN_SET)
        R = hn
        free_hn = everything()
        t_R = out_product([[D["w_o"][n]] for n in range(2)], 4, 8, lambda k: M[:, k * 512:(k + 1) * 512], 512,
                          lambda n, b, t: acopy(R[:, n * 512:(n + 1) * 512], ps[:, b, :], t, free_hn), t_M)
        t = norm_to(R, R, 8, V("post_mix"), 1024.0, t_R)
        for k in range(8):
            x = X[:, k * 512:(k + 1) * 512]
            t_x = vtt(x, x, R[:, k * 512:(k + 1) * 512], ADD)
        t_hn = norm_to(hn, X, 8, V("pre_ffn"), 1024.0, t_x)

        top[0] = mark_d - 0
        start = everything()
        A = take(22 * 512)
        up = [take(514) for _ in range(4)]
        zb = [take(512) for _ in range(4)]
        for x in range(4):
            t_up0 = pool.do(lambda e, x=x: e.memset(up[x][:, 0:2], 0.0), start)
        t_up = [t_up0] * 4
        t_zb = [start] * 4
        zs = {}

        def use_up(n, b, t):
            x = n % 4
            tile_ = 2 * (n // 4) + x % 2 + (22 if x >= 2 else 0)
            r = acopy(up[x][:, 2:514], ps[:, b, :], t, t_up[x])
            z = zb[x]
            vts(z, up[x][:, 0:512], V("conv_w", 3 * tile_, 3 * tile_ + 1), V("conv_b", tile_, tile_ + 1), MUL, ADD,
                r, t_up0, t_zb[x])
            vstt(z, up[x][:, 1:513], V("conv_w", 3 * tile_ + 1, 3 * tile_ + 2), z, MUL, ADD)
            t2 = vstt(z, up[x][:, 2:514], V("conv_w", 3 * tile_ + 2, 3 * tile_ + 3), z, MUL, ADD)
            t_up[x] = t2
            if x < 2:
                zs[x] = aact(z, z, ACT.Silu, t2)
            else:
                a = 2 * (n // 4) + x % 2
                t2 = vtt(A[:, a * 512:(a + 1) * 512], zb[x - 2], z, MUL, zs[x - 2])
                t_zb[x] = t_zb[x - 2] = t2
                t_A[0] = t2
            return r

        t_A = [None]
        out_product([[D["w_up"][n]] for n in range(11)], 4, 8, hk, 512, use_up, t_hn)
        table(LN_SET)
        free_hn = everything()
        t_R = out_product([[D["w_down"][n]] for n in range(8)], 1, 22, lambda k: A[:, k * 512:(k + 1) * 512], 512,
                          lambda n, b, t: acopy(R[:, n * 512:(n + 1) * 512], ps[:, b, :], t, free_hn), t_A[0])
        t = norm_to(R, R, 8, V("post_ffn"), 1024.0, t_R)
        s_out = dsem("s_out")
        for k in range(8):
            x = X[:, k * 512:(k + 1) * 512]
            t = vtt(x, x, R[:, k * 512:(k + 1) * 512], ADD)
            t_out = sp.dma(s_out, D["out"][:, k * 512:(k + 1) * 512], x, t)
        sp.wait(t_out)
        finish_block()


def _tiles(w, width):
    k, n = w.shape
    v = w.reshape(k // 128, 128, n // width, width).transpose(2, 1, 0, 3)
    return np.ascontiguousarray(v).reshape(n // width, 128, k // 128 * width)


def _cols(v):
    return v.reshape(-1, 128).T


def _feat(x):
    t, f = x.shape
    return np.ascontiguousarray(x.T.reshape(f // 128, 128, t).transpose(1, 0, 2)).reshape(128, -1)


def layout(a):
    D = {}
    D["consts"] = constants()
    D["axial"] = axial_tables()
    D["bias"] = bias_tables()
    dn = a["dn_w_in"][0]
    q, k, v = dn[:, 0:1024], dn[:, 1024:2048], dn[:, 2048:4096]
    z = dn[:, 4096:6144]
    groups = [np.concatenate([x[:, j * n:(j + 1) * n] for x, n in ((q, 128), (k, 128), (v, 256))], 1)
              for j in range(8)]
    D["w_dn"] = np.concatenate([_tiles(g, 512) for g in groups])
    D["w_z"] = _tiles(z, 256)
    D["w_ab"] = _tiles(dn[:, 6144:6208], 64)[0]
    cw = a["dn_conv_w"][0].reshape(5, 32, 128)
    order = [t for j in range(8) for t in (j, 8 + j, 16 + 2 * j, 17 + 2 * j)]
    conv = cw[:, order, :].transpose(2, 1, 0).reshape(128, 160)
    cvec = np.stack([_cols(a["c"][0]), _cols(a["c_ctx"])], 2).reshape(128, 16)
    vecs = {
        "ada_b": np.concatenate([_cols(a["ada_b"][i]) for i in range(2)], 1),
        "norm_g": np.concatenate([_cols(a["norm_g"][i]) for i in range(2)], 1),
        "conv": conv, "cvec": cvec, "final_g": _cols(a["final_norm_g"]),
        "qn_g": _cols(a["att_q_norm_g"][0]), "kn_g": _cols(a["att_k_norm_g"][0]),
        "pre_mix": _cols(a["g_pre_mix_2"][0]), "b_gate": _cols(a["b_gate_2"][0]),
        "mla_q": _cols(a["mla_q_norm_2"][0]), "mla_kv": _cols(a["mla_kv_norm_2"][0]),
        "g_mem": _cols(a["g_mem_2"][0]), "post_mix": _cols(a["g_post_mix_2"][0]),
        "pre_ffn": _cols(a["g_pre_ffn_2"][0]), "conv_b": _cols(a["conv_b_2"][0]),
        "conv_w": a["conv_w_2"][0].reshape(3, 44, 128).transpose(2, 1, 0).reshape(128, 132),
        "post_ffn": _cols(a["g_post_ffn_2"][0]),
    }
    D["vecs"] = np.concatenate([vecs[n] for n in VECS], 1)
    assert D["vecs"].shape == (128, NVEC)
    D["ada_w"] = np.concatenate([_tiles(a["ada_w"][i], 512) for i in range(2)])
    D["xT"] = _feat(np.concatenate([a["ctx"][0], a["x"][0]], 0))
    D["dt_bias"] = a["dn_dt_bias"][0].reshape(32)
    D["a_log"] = a["dn_a_log"][0].reshape(32)
    D["o_norm_g"] = a["dn_o_norm_g"][0]
    D["dn_out"] = _tiles(a["dn_w_out"][0], 256)
    D["att_in"] = _tiles(a["att_w_in"][0], 512)
    D["att_out"] = _tiles(a["att_w_out"][0], 512)
    w = a["w_in_2"][0]
    D["w_cq"] = _tiles(w[:, 0:384], 384)[0]
    D["w_ckv"] = _tiles(w[:, 384:640], 256)[0]
    D["w_kr"] = _tiles(w[:, 640:672], 32)[0]
    D["w_dil"] = _tiles(w[:, 672:5280], 512)
    D["w_memq"] = _tiles(w[:, 5280:5792], 512)[0]
    D["w_gate"] = _tiles(w[:, 5792:8864], 512)
    D["w_uq"] = _tiles(a["w_uq_2"][0], 768)[0]
    ukv = a["w_ukv_2"][0].reshape(256, 8, 128)
    D["w_uk"] = _tiles(ukv[:, :, 0:64].reshape(256, 512), 512)[0]
    D["w_uv"] = _tiles(ukv[:, :, 64:128].reshape(256, 512), 512)[0]
    D["w_memkv"] = _tiles(a["w_mem_kv_2"][0], 512)
    D["memT"] = _feat(a["mem_2"][0])
    D["positions"] = a["positions_2"][0]
    D["w_br"] = np.stack([_tiles(a[n][0], 1024)[0] for n in ("w_br_mla_2", "w_br_dil_2", "w_br_mem_2")])
    D["w_o"] = _tiles(a["w_o_2"][0], 512)
    up = a["w_ffn_up_2"][0]
    D["w_up"] = _tiles(np.concatenate([up[:, s + 256 * n:s + 256 * n + 256] for n in range(11)
                                       for s in (0, 2816)], 1), 512)
    D["w_down"] = _tiles(a["w_ffn_down_2"][0], 128)
    return {n: np.ascontiguousarray(x) for n, x in D.items()}


_SCRATCH = (8, 128, 1536)


def kernel(**inputs):
    import concourse.bacc as bacc
    from concourse.bass_utils import run_bass_kernel_spmd

    arrays = layout({n: np.asarray(v) for n, v in inputs.items()})
    nc = bacc.Bacc("TRN2", target_bir_lowering=False, num_devices=1)
    D = {n: nc.dram_tensor(f"in_{n}", a.shape, mybir.dt.from_np(a.dtype), kind="ExternalInput").ap()
         for n, a in arrays.items()}
    D["scratch"] = nc.dram_tensor("scratch", _SCRATCH, F32, kind="Internal").ap()
    D["out"] = nc.dram_tensor("out_y", (128, 4096), F32, kind="ExternalOutput").ap()
    program(nc, D)
    r = run_bass_kernel_spmd(nc, [{f"in_{n}": a for n, a in arrays.items()}], core_ids=[0])
    y = np.asarray(r.results[0]["out_y"])
    return np.ascontiguousarray(y.reshape(128, 8, 512).transpose(2, 1, 0)).reshape(1, 512, 1024)
```
